# Optimizing a Trainium2 kernel written in Bass

```python
import jax, jax.numpy as jnp
from jax import lax
import numpy as np

D_MODEL = 2048
BATCH = 1
SEQ = 256
DEPTH = 2
DEC_BATCH = 8
DEC_SEQ = 4
PAST_LEN = 256
PAGE_SIZE = 128

CONV_CH = D_MODEL // 2
CONV_WIDTH = 3
HEAD_DIM = 128
N_HEADS = (D_MODEL - CONV_CH) // HEAD_DIM
N_KV = 2
GQA = N_HEADS // N_KV
ATT_W = N_HEADS * HEAD_DIM
KV_W = N_KV * HEAD_DIM
CMP_LEN = 32
CMP_STRIDE = 16
SEL_BLOCK = 64
N_SELECT = 8
WINDOW = 512
Q_BLOCK = 128
ROPE_THETA = 10000.0
EPS = 1e-6
NEG = -1e30
FORCE_SCORE = 1e3
N_BRANCH_KV = 4

_IN_SIZES = (CONV_CH, CONV_CH, CONV_CH, CONV_CH, ATT_W, KV_W, KV_W, KV_W, KV_W, KV_W, KV_W, 3 * N_HEADS, ATT_W)
_IN_OFFS = tuple(sum(_IN_SIZES[:i]) for i in range(len(_IN_SIZES) + 1))
N_IN = _IN_OFFS[-1]

kernel_name = 'nsa_shortconv_parallel_hybrid_step'

def rmsnorm(x, g):
    xf = x.astype(jnp.float32)
    y = xf * lax.rsqrt(jnp.mean(xf * xf, -1, keepdims=True) + EPS)
    return (y * g.astype(jnp.float32)).astype(x.dtype)

def rope(x, pos):
    half = HEAD_DIM // 2
    inv = jnp.power(ROPE_THETA, -jnp.arange(half, dtype=jnp.float32) / half)
    ang = pos.astype(jnp.float32)[:, None] * inv
    shp = (1, ang.shape[0]) + (1,) * (x.ndim - 3) + (half,)
    cos, sin = jnp.cos(ang).reshape(shp), jnp.sin(ang).reshape(shp)
    xf = x.astype(jnp.float32)
    x1, x2 = xf[..., :half], xf[..., half:]
    return jnp.concatenate([x1 * cos - x2 * sin, x2 * cos + x1 * sin], -1).astype(x.dtype)

def _masked_softmax(s, mask):
    s = jnp.where(mask, s.astype(jnp.float32), NEG)
    e = jnp.where(mask, jnp.exp(s - jnp.max(s, -1, keepdims=True)), 0.0)
    return e / jnp.maximum(jnp.sum(e, -1, keepdims=True), 1e-30)

def _modulated_projection(x, c, w_ada, b_ada, g_pre, w_in):
    mod = jax.nn.silu(c) @ w_ada + b_ada
    shift, scale, gate = jnp.split(mod, 3, axis=-1)
    h = rmsnorm(x, g_pre) * (1.0 + scale[:, None]) + shift[:, None]
    return h @ w_in, gate

def _split(u):
    return [u[..., _IN_OFFS[i]:_IN_OFFS[i + 1]] for i in range(len(_IN_SIZES))]

def _short_conv(b_g, c_g, x_in, z, buf, conv_w):
    u = c_g * x_in
    t = u.shape[1]
    up = jnp.concatenate([buf.astype(u.dtype), u], axis=1)
    y = sum(conv_w[i] * up[:, i:i + t] for i in range(CONV_WIDTH))
    return jax.nn.silu(z) * (b_g * y), up[:, -(CONV_WIDTH - 1):]

def _attn_streams(parts, pos):
    q, kc, vc, ks, vs, kw, vw, g, z = parts[4:]
    bsz, t = q.shape[:2]
    q = rope(q.reshape(bsz, t, N_KV, GQA, HEAD_DIM), pos)
    kv = lambda a: a.reshape(bsz, t, N_KV, HEAD_DIM)
    kc, ks, kw = rope(kv(kc), pos), rope(kv(ks), pos), rope(kv(kw), pos)
    gates = jax.nn.sigmoid(g.reshape(bsz, t, N_KV, GQA, 3))
    return q, kc, kv(vc), ks, kv(vs), kw, kv(vw), gates, z

def _compress(k, pe, w1, w2):
    bsz, length = k.shape[:2]
    nsub = -(-length // CMP_STRIDE)
    r = CMP_LEN // CMP_STRIDE
    k = jnp.pad(k, ((0, 0), (0, nsub * CMP_STRIDE - length), (0, 0), (0, 0)))
    sub = k.reshape(bsz, nsub, CMP_STRIDE, N_KV, HEAD_DIM)
    nc = nsub - r + 1
    blocks = jnp.concatenate([sub[:, i:i + nc] for i in range(r)], axis=2)
    blocks = blocks + pe[:, None, :]
    flat = blocks.transpose(0, 1, 3, 2, 4).reshape(bsz, nc, N_KV, CMP_LEN * HEAD_DIM)
    return jax.nn.silu(flat @ w1) @ w2

def _n_sel_blocks(length):
    return max(-(-length // SEL_BLOCK), N_SELECT)

def _sel_blocks(k, nb):
    bsz, length = k.shape[:2]
    k = jnp.pad(k, ((0, 0), (0, nb * SEL_BLOCK - length), (0, 0), (0, 0)))
    return k.reshape(bsz, nb, SEL_BLOCK, N_KV, HEAD_DIM).transpose(0, 3, 1, 2, 4)

def _nsa_attend(q, qpos, kc, vc, kb, vb, kw, vw, kw_pos, gates):
    scale = HEAD_DIM ** -0.5
    bsz, tq = q.shape[:2]
    nc, nb = kc.shape[1], kb.shape[2]
    c_end = jnp.arange(nc) * CMP_STRIDE + (CMP_LEN - 1)
    s = jnp.einsum('btgrd,bcgd->bgrtc', q, kc) * scale
    p_cmp = _masked_softmax(s, c_end[None, :] <= qpos[:, None])
    o_cmp = jnp.einsum('bgrtc,bcgd->btgrd', p_cmp.astype(vc.dtype), vc)
    per = SEL_BLOCK // CMP_STRIDE
    imp = jnp.pad(p_cmp.sum(2), ((0, 0), (0, 0), (0, 0), (0, nb * per - nc)))
    imp = imp.reshape(bsz, N_KV, tq, nb, per).sum(-1)
    blk = jnp.arange(nb)
    cur = (qpos // SEL_BLOCK)[:, None]
    forced = (blk == 0) | (blk == cur) | (blk == cur - 1)
    score = jnp.where(blk <= cur, jnp.where(forced, FORCE_SCORE, imp), NEG)
    top_s, top_i = lax.top_k(score, N_SELECT)
    take = jax.vmap(jax.vmap(lambda a, i: a[i]))
    k_sel, v_sel = take(kb, top_i), take(vb, top_i)
    k_pos = top_i[..., None] * SEL_BLOCK + jnp.arange(SEL_BLOCK)
    m_sel = (top_s > 0.5 * NEG)[..., None] & (k_pos <= qpos[:, None, None])
    s = jnp.einsum('btgrd,bgtnkd->bgrtnk', q, k_sel) * scale
    p = _masked_softmax(s.reshape(s.shape[:4] + (-1,)), m_sel.reshape(bsz, N_KV, 1, tq, -1))
    o_slc = jnp.einsum('bgrtj,bgtjd->btgrd', p.astype(v_sel.dtype),
                       v_sel.reshape(bsz, N_KV, tq, -1, HEAD_DIM))
    s = jnp.einsum('btgrd,bwgd->bgrtw', q, kw) * scale
    dist = qpos[:, None] - kw_pos[None, :]
    p = _masked_softmax(s, (dist >= 0) & (dist < WINDOW) & (kw_pos[None, :] >= 0))
    o_win = jnp.einsum('bgrtw,bwgd->btgrd', p.astype(vw.dtype), vw)
    return gates[..., 0:1] * o_cmp + gates[..., 1:2] * o_slc + gates[..., 2:3] * o_win

def _prompt_nsa(q, kc, vc, kb, vb, kw, vw, gates):
    bsz, t = q.shape[:2]
    pad = ((0, 0), (WINDOW, 0), (0, 0), (0, 0))
    kw_pad, vw_pad = jnp.pad(kw, pad), jnp.pad(vw, pad)

    def block(i):
        s0 = i * Q_BLOCK
        sl = lambda a, n: lax.dynamic_slice_in_dim(a, s0, n, axis=1)
        qpos = s0 + jnp.arange(Q_BLOCK)
        kpos = s0 - WINDOW + jnp.arange(WINDOW + Q_BLOCK)
        return _nsa_attend(sl(q, Q_BLOCK), qpos, kc, vc, kb, vb,
                           sl(kw_pad, WINDOW + Q_BLOCK), sl(vw_pad, WINDOW + Q_BLOCK), kpos,
                           sl(gates, Q_BLOCK))

    o = lax.map(block, jnp.arange(t // Q_BLOCK))
    return jnp.moveaxis(o, 0, 1).reshape(bsz, t, N_KV, GQA, HEAD_DIM)

def _merge(x, ya, yb, gate, g_grp, w_out, g_post):
    y = jnp.concatenate([rmsnorm(ya, g_grp[:CONV_CH]), rmsnorm(yb, g_grp[CONV_CH:])], -1) @ w_out
    return x + gate[:, None] * rmsnorm(y, g_post)

def setup_inputs(seed: int = 0) -> dict:
    key = jax.random.key(seed)
    ks = jax.random.split(key, 19)
    n_pages = PAST_LEN // PAGE_SIZE
    n_used = DEC_BATCH * n_pages
    n_pool = n_used + n_used // 4
    wbuf = min(WINDOW, PAST_LEN)
    nrm = lambda k, shape, s: s * jax.random.normal(k, shape, jnp.float32)
    page_table = jax.random.permutation(ks[0], n_pool)[:n_used].reshape(DEC_BATCH, n_pages).astype(jnp.int32)
    return {
        'x_prompt': nrm(ks[1], (BATCH, SEQ, D_MODEL), 1.0),
        'x_sample': nrm(ks[2], (DEC_BATCH, DEC_SEQ, D_MODEL), 1.0),
        'cache_kv': nrm(ks[3], (DEPTH, n_pool, PAGE_SIZE, N_BRANCH_KV, N_KV, HEAD_DIM), 1.0),
        'cache_win': nrm(ks[4], (DEPTH, DEC_BATCH, wbuf, 2, N_KV, HEAD_DIM), 1.0),
        'state_conv': nrm(ks[5], (DEPTH, DEC_BATCH, CONV_WIDTH - 1, CONV_CH), 1.0),
        'page_table': page_table,
        'c_prompt': nrm(ks[6], (BATCH, D_MODEL), 1.0),
        'c_sample': nrm(ks[7], (DEC_BATCH, D_MODEL), 1.0),
        'w_ada': nrm(ks[8], (DEPTH, D_MODEL, 3 * D_MODEL), D_MODEL ** -0.5),
        'b_ada': nrm(ks[9], (DEPTH, 3 * D_MODEL), 0.01),
        'g_pre': 1.0 + nrm(ks[10], (DEPTH, D_MODEL), 0.1),
        'w_in': nrm(ks[11], (DEPTH, D_MODEL, N_IN), D_MODEL ** -0.5),
        'conv_w': nrm(ks[12], (DEPTH, CONV_WIDTH, CONV_CH), CONV_WIDTH ** -0.5),
        'cmp_pe': nrm(ks[13], (DEPTH, 2, CMP_LEN, HEAD_DIM), 0.1),
        'cmp_w1': nrm(ks[14], (DEPTH, 2, CMP_LEN * HEAD_DIM, HEAD_DIM), (CMP_LEN * HEAD_DIM) ** -0.5),
        'cmp_w2': nrm(ks[15], (DEPTH, 2, HEAD_DIM, HEAD_DIM), HEAD_DIM ** -0.5),
        'g_grp': 1.0 + nrm(ks[16], (DEPTH, D_MODEL), 0.1),
        'w_out': nrm(ks[17], (DEPTH, CONV_CH + ATT_W, D_MODEL), D_MODEL ** -0.5),
        'g_post': 1.0 + nrm(ks[18], (DEPTH, D_MODEL), 0.1),
    }

def reference(x_prompt, x_sample, cache_kv, cache_win, state_conv, page_table, c_prompt, c_sample,
              w_ada, b_ada, g_pre, w_in, conv_w, cmp_pe, cmp_w1, cmp_w2, g_grp, w_out, g_post):
    bp, tp = x_prompt.shape[:2]
    bs, ts = x_sample.shape[:2]
    past = page_table.shape[1] * cache_kv.shape[2]
    wbuf = cache_win.shape[2]
    pos_p = jnp.arange(tp)
    pos_s = past + jnp.arange(ts)
    kw_pos_s = past - wbuf + jnp.arange(wbuf + ts)
    nb_p, nb_s = _n_sel_blocks(tp), _n_sel_blocks(past + ts)
    xp, xs = x_prompt, x_sample
    kv_p, kv_s, win_p, win_s, conv_p, conv_s = [], [], [], [], [], []
    for l in range(DEPTH):
        comp = lambda k, i: _compress(k, cmp_pe[l, i], cmp_w1[l, i], cmp_w2[l, i])
        u, gate = _modulated_projection(xp, c_prompt, w_ada[l], b_ada[l], g_pre[l], w_in[l])
        parts = _split(u)
        ya, cbuf = _short_conv(*parts[:4], jnp.zeros((bp, CONV_WIDTH - 1, CONV_CH), xp.dtype), conv_w[l])
        q, kc, vc, ksl, vsl, kw, vw, gates, z = _attn_streams(parts, pos_p)
        o = _prompt_nsa(q, comp(kc, 0), comp(vc, 1), _sel_blocks(ksl, nb_p), _sel_blocks(vsl, nb_p), kw, vw, gates)
        yb = o.reshape(bp, tp, ATT_W) * jax.nn.silu(z)
        xp = _merge(xp, ya, yb, gate, g_grp[l], w_out[l], g_post[l])
        kv_p.append(jnp.stack([kc, vc, ksl, vsl], axis=2))
        win_p.append(jnp.stack([kw, vw], axis=2)[:, -min(WINDOW, tp):])
        conv_p.append(cbuf)
        u, gate = _modulated_projection(xs, c_sample, w_ada[l], b_ada[l], g_pre[l], w_in[l])
        parts = _split(u)
        ya, cbuf = _short_conv(*parts[:4], state_conv[l], conv_w[l])
        q, kc, vc, ksl, vsl, kw, vw, gates, z = _attn_streams(parts, pos_s)
        new_kv = jnp.stack([kc, vc, ksl, vsl], axis=2)
        past_kv = cache_kv[l, page_table].reshape(bs, past, N_BRANCH_KV, N_KV, HEAD_DIM)
        full = jnp.concatenate([past_kv.astype(new_kv.dtype), new_kv], axis=1)
        win = jnp.concatenate([cache_win[l].astype(kw.dtype), jnp.stack([kw, vw], axis=2)], axis=1)
        o = _nsa_attend(q, pos_s, comp(full[:, :, 0], 0), comp(full[:, :, 1], 1),
                        _sel_blocks(full[:, :, 2], nb_s), _sel_blocks(full[:, :, 3], nb_s),
                        win[:, :, 0], win[:, :, 1], kw_pos_s, gates)
        yb = o.reshape(bs, ts, ATT_W) * jax.nn.silu(z)
        xs = _merge(xs, ya, yb, gate, g_grp[l], w_out[l], g_post[l])
        kv_s.append(new_kv)
        win_s.append(win[:, -wbuf:])
        conv_s.append(cbuf)
    return (xp, xs, jnp.stack(kv_p), jnp.stack(kv_s), jnp.stack(win_p), jnp.stack(win_s),
            jnp.stack(conv_p), jnp.stack(conv_s))


_drawn_inputs = setup_inputs


def setup_inputs(seed=0):
    import zlib

    import numpy as np

    out = dict(_drawn_inputs(seed))
    spreads = {}
    factors = {'b_ada': 2.777}
    for name, (base, spread) in spreads.items():
        noise = np.random.default_rng([zlib.crc32(name.encode()), seed]).standard_normal(out[name].shape)
        drawn = base * np.exp(spread * noise) if base else spread * noise
        out[name] = __import__('jax').numpy.asarray(drawn.astype(out[name].dtype))
    for name, factor in factors.items():
        out[name] = (out[name] * factor).astype(out[name].dtype)
    return out
```

```python
from contextlib import ExitStack

import concourse.bass as bass
from concourse import mybir
import numpy as np

F32 = mybir.dt.float32
F32R = mybir.dt.float32r
ALU = mybir.AluOpType
ACT = mybir.ActivationFunctionType
AX_X = mybir.AxisListType.X

P = 128
DEPTH, DM, SEQ, NB, TS = 2, 2048, 256, 8, 4
KT = DM // P
NTS = NB * TS
T = SEQ + NTS
PAST, PAGE = 256, 128
NC_CONV, NH, NKV, HD = 1024, 8, 2, 128
GQA = NH // NKV
N_IN = 4 * NC_CONV + NH * HD + 6 * NKV * HD + 3 * NH + NH * HD
COL_Q, COL_KV = 4 * NC_CONV, 4 * NC_CONV + NH * HD
COL_G = COL_KV + 6 * NKV * HD
COL_Z = COL_G + 3 * NH
NG = 3 * NH
CMP_LEN, STRIDE, NBLK = 32, 16, 15
NSEQ = NB * NKV
NROW = T // STRIDE + NBLK
ROWS = 1 + NB
EPS, NEG = 1e-6, -1e30
SCALE = float(HD) ** -0.5
CH = 2 * P
N_SELECT, SEL_BLOCK, WINDOW = 8, 64, 512
assert max(-(-SEQ // SEL_BLOCK), N_SELECT) == N_SELECT == max(-(-(PAST + TS) // SEL_BLOCK), N_SELECT)
assert WINDOW > PAST + TS and (NBLK * STRIDE + CMP_LEN - 1) > PAST + TS - 1

C_ID, C_COS, C_SIN, C_TRI = 0, P, P + T, P + 2 * T
C_CMP = C_TRI + P
C_NEW = C_CMP + 2 * NBLK
C_GM = C_NEW + 4 * NTS
C_SUM = C_GM + NG
C_END = C_SUM + ROWS


def shape_constants():
    c = np.zeros((P, C_END), np.float32)
    c[:, C_ID:C_ID + P] = np.eye(P)
    half = HD // 2
    inv = np.power(np.float32(10000.0), -np.arange(half, dtype=np.float32) / np.float32(half))
    pos = np.concatenate([np.arange(SEQ), np.tile(PAST + np.arange(TS), NB)]).astype(np.float32)
    ang = (pos[None, :] * inv[:, None]).astype(np.float32)
    c[:, C_COS:C_COS + T] = np.concatenate([np.cos(ang), np.cos(ang)])
    c[:, C_SIN:C_SIN + T] = np.concatenate([np.sin(ang), -np.sin(ang)])
    r = np.arange(P)
    c[:, C_TRI:C_TRI + P] = np.where(r[None, :] <= r[:, None], 0.0, NEG)
    for i in range(2):
        ends = np.arange(NBLK) * STRIDE + CMP_LEN - 1
        c[:, C_CMP + i * NBLK:C_CMP + (i + 1) * NBLK] = np.where(ends[None, :] <= r[:, None] + i * P, 0.0, NEG)
    for p in range(4):
        for q in range(NTS):
            b, t = q // TS, q % TS
            ok = (b == 2 * p + r // 64) & (t <= r % TS)
            c[:, C_NEW + p * NTS + q] = np.where(ok, 0.0, NEG)
    for col in range(NG):
        head = col // 3
        c[:, C_GM + col] = (head == ((r // 32) % 2) * GQA + (r % 32) // TS) & (r % 32 < GQA * TS)
    for i in range(2 * ROWS):
        c[i, C_SUM + i % ROWS] = 1.0
    return c


class Counts:

    def __init__(self, eng, sems, per):
        self.eng, self.sems, self.per = eng, sems, per
        self.n = {}
        self.loops = []

    def value(self, name):
        v = self.n.get(name, 0)
        for loop, i in self.loops:
            k = self.per.get((name, loop), 0)
            if k:
                v = i * k + v
        return v

    def take(self, name, k=1):
        self.n[name] = self.n.get(name, 0) + k
        return self.sems[name], self.value(name)

    def give(self, name, k=1):
        self.n[name] = self.n.get(name, 0) + k
        return self.sems[name], k

    def same(self, name):
        return self.sems[name], self.value(name)

    def ahead(self, name, k=1):
        return self.sems[name], self.value(name) + k

    def skip(self, name, k=1):
        self.n[name] = self.n.get(name, 0) + k

    def enter(self, loop, i):
        self.loops.append((loop, i))
        return dict(self.n)

    def leave(self, loop, before, trips):
        self.loops.pop()
        for name in self.n:
            d = self.n[name] - before.get(name, 0)
            known = self.per.setdefault((name, loop), d)
            assert known == d, (name, loop, known, d)
            self.n[name] = before.get(name, 0) + trips * d


PROMPT = {s: (s // 3, s % 3) for s in range(12)}
SAMPLE = {0: (0, 0), 2: (0, 1), 4: (0, 2), 7: (1, 0), 9: (1, 1), 11: (1, 2)}
KTURN = {s: pk for s, pk in SAMPLE.items() if pk[1] < 2}
VTURN = {s: pk for s, pk in SAMPLE.items() if pk[1] == 2}
GATE = (1, 2, 0)

SEMS = """crow0 crow1 crow_used w1_in0 w1_in1 w1_used apart a_done act_step av_ready b_done bank0 bank1 c_done c_in c_tanh cache0 cache1 cache2 cache3 cache_used cmp_a
cmp_h cmp_row cmp_put cmp_tanh const_in dve_step fin_put gate_ready graw h_hi h_ready h_s hi_ready kc_got kc_put
kv_done lo_ready mem_set misc_got misc_put mod_row op_got op_put os_got os_put pool_step pt_got pt_put pts_got
pts_put qc_ready qs_ready raw0 raw1 sp_e sp_nm sp_p sp_put sq_free ss_e ss_nm ss_p ss_put ssq_ready stored
stored2 tile_done tp_got tp_put u_put v_ready v_turn vec_in x_back x_in x_put x_spill x_tile xn y_done y_f
y_hi y_hl y_sq ya_ready yb_ready z_t""".split()


def program(nc, per, ins, outs, consts, spill):
    (x_prompt, x_sample, cache_kv, cache_win, state_conv, page_table, c_prompt, c_sample, w_ada, b_ada, g_pre,
     w_in, conv_w, cmp_pe, cmp_w1, cmp_w2, g_grp, w_out, g_post) = ins
    y_p, y_s, kv_p, kv_s, win_p, win_s, conv_p, conv_s = outs

    with ExitStack() as ctx:
        def sb(name, shape, dt=F32):
            return ctx.enter_context(nc.sbuf_tensor(name, shape, dt))

        raw = sb("raw", [P, 2, KT * CH])
        w_hi = sb("w_hi", [P, 2, KT, P], F32R)
        w_lo = sb("w_lo", [P, 2, KT, P], F32R)
        xT = sb("xT", [P, KT * T])
        h_hi = sb("h_hi", [P, KT, T], F32R)
        h_lo = sb("h_lo", [P, KT, T], F32R)
        mix = sb("mix", [P, KT, T])
        heads = sb("heads", [P, 8 * T + 2 * T + 448 + 6 * CH])
        lent = sb("lent", [P, 2 * CMP_LEN // 4 * P + 2048])
        stage = sb("stage", [P, 3, CH])
        cbuf = sb("cbuf", [P, 2, T])
        ubuf = sb("ubuf", [P, 2, 2 + SEQ + NB * (TS + 2)])
        gz = sb("gz", [P, 2, T])
        qs = sb("qs", [P, 4, 32])
        cst = sb("cst", [P, C_END])
        ones = sb("ones", [P, P])
        vec = sb("vec", [P, 120])
        w2 = sb("w2", [P, 2, P])
        mod = sb("mod", [P, 48, ROWS])
        cHL = sb("cHL", [P, KT, 2 * ROWS], F32R)
        kcT = sb("kcT", [P, (NSEQ + 2) * NBLK])
        cact = sb("cact", [P, 2, (NSEQ + 2) * NBLK])
        vcs = sb("vcs", [NBLK, 4, P])
        vcp = sb("vcp", [NBLK, P])
        avc = sb("avc", [P, 9 * NBLK])
        stT = sb("stT", [P, 8, 2 * NB])
        uo = sb("uo", [P, 8, 2 + 2 * NB])
        acc = sb("acc", [P, T])
        sqp = sb("sqp", [P, T])
        rs = sb("rs", [P, T])
        gtok = sb("gtok", [P, 2, NG])
        gsm = sb("gsm", [P, 4, 3])
        mrow = sb("mrow", [2 * ROWS, 2, P])
        small = sb("small", [P, 16])
        pages = sb("pages", [1, NB * 2], mybir.dt.int32)

        kvf = heads[:, 0:8 * T]
        kvT = kvf.rearrange("p (k t) -> p k t", t=T)
        vq = heads[:, 8 * T:10 * T + 448]
        vtok = heads[:, 10 * T + 448:].rearrange("p (b i d) -> p b i d", b=2, i=3)
        X = lent[:, 0:8 * PAGE].rearrange("p (a b) -> p a b", a=4)
        prob = lent[:, 1024:1792].rearrange("p (a b) -> p a b", a=2)
        sprobT, probT, sprob = lent[:, 1792:2176], lent[:, 2176:2560], lent[:, 2560:2560 + T]
        mixf = mix[:, :, :].rearrange("p k t -> p (k t)")
        ring = xT[:, 0:4096].rearrange("p (s g d) -> p s g d", s=4, g=2)
        graw = xT[:, 4096:4096 + KT * NG].rearrange("p (k n) -> p k n", k=KT)
        xv = xT[:, :].rearrange("p (k t) -> p k t", k=KT)
        rawv = [raw[:, s, :].rearrange("p (k n) -> p k n", k=KT) for s in range(2)]
        w1v = [raw[:, s, :].rearrange("p (j n) -> p j n", j=CMP_LEN) for s in range(2)]
        past = [mixf[:, 0:17 * 2 * PAGE], heads[:, 0:17 * 2 * PAGE]]
        past = [a.rearrange("p (q t) -> p q t", t=2 * PAGE) for a in past]
        w1s = lent[:, 0:2048].rearrange("p (j n) -> p j n", n=P)
        crow = lent[:, 2048:4096].rearrange("p (s g d) -> p s g d", s=2, g=2)
        vtmp = vq[:, 0:2 * T].rearrange("p (s t) -> p s t", s=2)
        vcur = vq[:, 0:512].rearrange("p (b i d) -> p b i d", b=2, i=2)
        qc = vq[:, 512:1024].rearrange("p (s t) -> p s t", s=2)
        kwork = X
        ident = cst[:, C_ID:C_ID + P]
        tri = cst[:, C_TRI:C_TRI + P]
        eps = small[:, 15:16]
        xsrow = X[0:2 * NB, 0:4, :].rearrange("p a b -> p (a b)")

        uorow = X[0:2 + 2 * NB, 0:4, :].rearrange("p a b -> p (a b)")

        ps = [ctx.enter_context(nc.psum_tensor(f"ps{i}", [P, 512], F32)) for i in range(8)]
        proj = [ps[0], ps[1]]
        pmisc, ptr, pS, pSs, pPT, pO = ps[2], ps[3], ps[4], ps[5], ps[6], ps[7]
        pOs = pmisc

        sems = {n: ctx.enter_context(nc.semaphore(n)) for n in SEMS}
        block = ctx.enter_context(nc.Block())

        def apart(eng):
            eng.sem_inc(sems["apart"], 1)

        class Loop:

            def __init__(self, eng, c, name, trips):
                self.eng, self.c, self.name, self.trips = eng, c, name, trips

            def __enter__(self):
                apart(self.eng)
                self.f = self.eng.Fori(0, self.trips)
                i = self.f.__enter__()
                self.before = self.c.enter(self.name, i)
                return i

            def __exit__(self, *a):
                if a[0]:
                    return False
                self.c.leave(self.name, self.before, self.trips)
                return self.f.__exit__(*a)

        @block.sync
        def _(sp):
            c = Counts(sp, sems, per.setdefault("sp", {}))
            sp.dma_start(cst[:, :], consts).then_inc(*c.give("const_in", 16))
            for i in range(2):
                sp.dma_start(raw[:, 0, i * DM:(i + 1) * DM], x_prompt[0, i * P:(i + 1) * P, :]).then_inc(*c.give("x_in", 16))
            sp.dma_start(raw[0:NTS, 1, 0:DM], x_sample.rearrange("b t d -> (b t) d")).then_inc(*c.give("x_in", 16))
            sp.dma_start(raw[0:1, 1, DM:2 * DM], c_prompt).then_inc(*c.give("c_in", 16))
            sp.dma_start(raw[1:ROWS, 1, DM:2 * DM], c_sample).then_inc(*c.give("c_in", 16))
            sp.dma_start(pages[:, :], page_table.rearrange("b (o g) -> o (b g)", o=1)).then_inc(*c.give("const_in", 16))
            sp.wait_ge(*c.same("const_in"))

            def chunk(slot, src):
                sp.wait_ge(*c.take("lo_ready", 2))
                sp.dma_start(raw[:, slot, :], src).then_inc(*c.give(f"raw{slot}", 16))

            def wcols(w, l, col):
                return w[bass.ds(l, 1), :, bass.ds(col, CH)].rearrange("l (k p) n -> p (l k) n", p=P)

            def load_cache(l, b, slot, kind, sem):
                for pg in range(2):
                    if kind == "win":
                        src = cache_win[bass.ds(l, 1), bass.ds(b, 1), pg * PAGE:(pg + 1) * PAGE].rearrange(
                            "l b t c g d -> (l b t) (c g d)")
                    else:
                        apart(sp)
                        page = sp.value_load(pages[0:1, bass.ds(b * 2 + pg, 1)], min_val=0, max_val=cache_kv.shape[1] - 1)
                        lo = 0 if kind == "cmp" else 2
                        src = cache_kv[bass.ds(l, 1), bass.ds(page, 1), :, lo:lo + 2].rearrange(
                            "l n t c g d -> (l n t) (c g d)")
                    sp.dma_start((crow if kind == "cmp" else ring)[:, slot, pg, :], src).then_inc(*c.give(sem, 16))

            with Loop(sp, c, "layer", DEPTH) as l:
                for lo, src in ((0, b_ada), (48, g_pre), (64, g_grp), (80, g_post)):
                    n = src.shape[1] // P
                    sp.dma_start(stage[lo:lo + n, 0, 0:P], src[bass.ds(l, 1), :].rearrange(
                        "l (k p) -> (l k) p", p=P)).then_inc(*c.give("vec_in", 16))
                sp.dma_start(stage[96:120, 0, 0:P], conv_w[bass.ds(l, 1)].rearrange(
                    "l i (k p) -> (l i k) p", p=P)).then_inc(*c.give("vec_in", 16))
                sp.dma_start(stage[0:64, 1, 0:P], cmp_pe[bass.ds(l, 1)].rearrange("l i j d -> (l i j) d")).then_inc(
                    *c.give("vec_in", 16))
                sp.dma_start(xsrow, state_conv[bass.ds(l, 1)].rearrange("l b i n -> (l b i) n")).then_inc(*c.give("vec_in", 16))
                sp.dma_start(w2[:, :, :], cmp_w2[bass.ds(l, 1)].rearrange("l i k n -> k (l i) n")).then_inc(*c.give("vec_in", 16))
                with Loop(sp, c, "shift", 4) as i:
                    for s in range(2):
                        chunk(s, wcols(w_ada, l, i * 512 + s * CH))
                        sp.wait_ge(*c.take("crow_used"))
                        load_cache(l, i * 2 + s, s, "cmp", f"crow{s}")
                for t in range(16):
                    if t % 2 == 0:
                        chunk(t // 2 % 2, wcols(w_ada, l, DM + t * P))
                        i, j = t // 8, t % 8 * 4
                        if t > 2:
                            sp.wait_ge(*c.take("w1_used"))
                        sp.dma_start(w1s[:, j % 16:j % 16 + 8, :], cmp_w1[bass.ds(l, 1), i, j * P:(j + 8) * P].rearrange(
                            "l (j d) n -> d (l j) n", d=P)).then_inc(*c.give(f"w1_in{t // 2 % 2}", 16))
                sp.wait_ge(*c.take("ssq_ready"))
                sp.dma_start(spill, xT[:, :]).then_inc(*c.give("x_spill", 16))
                with Loop(sp, c, "ada2", 4) as i:
                    for s in range(2):
                        chunk(s, wcols(w_ada, l, i * 512 + s * CH + 2 * DM))
                for i in range(5):
                    for s in range(2):
                        chunk(s, wcols(w_in, l, COL_Q + (2 * i + s) * CH))
                        if i == 0 and s == 1:
                            sp.wait_ge(*c.same("x_spill"))
                            sp.wait_ge(*c.take("h_ready", 4))
                            sp.dma_start(graw, w_in[bass.ds(l, 1), :, COL_G:COL_G + NG].rearrange(
                                "l (k p) n -> p (l k) n", p=P)).then_inc(*c.give("graw", 16))
                for s in range(2):
                    sp.wait_ge(*c.take("lo_ready", 2))
                    for j in range(0, CMP_LEN, CMP_LEN // 4):
                        sp.dma_start(w1v[s][:, j:j + CMP_LEN // 4, :], cmp_w1[bass.ds(l, 1), s, j * P:(j + CMP_LEN // 4) * P].rearrange(
                            "l (j d) n -> d (l j) n", d=P)).then_inc(*c.give(f"raw{s}", 16))
                c.skip("lo_ready")
                with Loop(sp, c, "turn", 2) as g:
                    for m in range(2):
                        for kind, off in enumerate((1, 2, 3, 0)):
                            s = kind % 2
                            chunk(s, wcols(w_in, l, off * NC_CONV + g * 512 + m * CH))
                            if kind < 2:
                                for bb in range(2):
                                    if bb == 0:
                                        sp.wait_ge(*c.take("cache_used"))
                                    load_cache(l, g * 4 + m * 2 + bb, 2 * kind + bb, ("slc", "win")[kind], f"cache{2 * kind + bb}")
                for i in range(2):
                    for s in range(2):
                        chunk(s, wcols(w_in, l, COL_Z + (2 * i + s) * CH))
                sp.wait_ge(*c.ahead("cache_used", 2))
                sp.dma_start(xT[:, :], spill).then_inc(*c.give("x_back", 16))
                with Loop(sp, c, "out", 4) as i:
                    for s in range(2):
                        chunk(s, wcols(w_out, l, i * 512 + s * CH))
                c.skip("w1_used", 2)

        @block.tensor
        def _(pe):
            c = Counts(pe, sems, per.setdefault("pe", {}))
            mm, tr = nc.tensor.matmul, nc.tensor.transpose
            pe.wait_ge(*c.take("const_in", 32))
            pe.wait_ge(*c.take("x_in", 48))
            pe.wait_ge(*c.take("mem_set"))
            for k in range(KT):
                b = k % 2
                pe.wait_ge(*c.take(f"bank{b}"))
                for i in range(2):
                    tr(proj[b][:, i * P:(i + 1) * P], raw[:, 0, i * DM + k * P:i * DM + (k + 1) * P], ident)
                tr(proj[b][:, SEQ:T], raw[0:NTS, 1, k * P:(k + 1) * P], ident[0:NTS, 0:NTS]).then_inc(*c.give("x_put"))
            pe.wait_ge(*c.take("misc_got"))
            pe.wait_ge(*c.take("c_done"))
            for k in range(KT):
                last = tr(pmisc[:, k * ROWS:(k + 1) * ROWS], mixf[0:ROWS, k * P:(k + 1) * P], ident[0:ROWS, 0:ROWS])
            last.then_inc(*c.give("misc_put"))
            c.skip("lo_ready", 4)
            pe.sem_inc(*c.give("cache_used", 2))
            pe.sem_inc(*c.give("crow_used", 2))

            def tile(s, width=P):
                pe.wait_ge(*c.take("lo_ready"))
                pe.wait_ge(*c.take(f"bank{s}"))
                out = proj[s][0:width, 0:T]
                for k in range(KT):
                    mm(out, w_hi[:, s, k, 0:width], h_hi[:, k, :], start=(k == 0), stop=False)
                    mm(out, w_hi[:, s, k, 0:width], h_lo[:, k, :], start=False, stop=False)
                    last = mm(out, w_lo[:, s, k, 0:width], h_hi[:, k, :], start=False, stop=(k == KT - 1))
                last.then_inc(*c.give("tile_done"))

            def mod_tile(s):
                pe.wait_ge(*c.take("lo_ready"))
                for k in range(KT):
                    mm(proj[s][0:2 * ROWS, 0:P], cHL[:, k, :], w_hi[:, s, k, :], start=(k == 0), stop=False)
                    last = mm(proj[s][0:2 * ROWS, 0:P], cHL[:, k, :], w_lo[:, s, k, :], start=False, stop=(k == KT - 1))
                last.then_inc(*c.give("tile_done"))

            def mod_turn(j):
                pe.wait_ge(*c.take("mod_row"))
                last = mm(pmisc[:, j * ROWS:(j + 1) * ROWS], mrow[:, j % 2, :], cst[0:2 * ROWS, C_SUM:C_END],
                          start=True, stop=True)
                if j == 3:
                    last.then_inc(*c.give("misc_put"))

            def mod_tiles(before_turn=None):
                pe.wait_ge(*c.take("misc_got"))
                for j in range(4):
                    mod_tile(j % 2)
                    if before_turn:
                        before_turn(j)
                    if j:
                        mod_turn(j - 1)
                mod_turn(3)

            def past_turn(j):
                slot, is_v = j // 2, j % 2
                if j:
                    pe.wait_ge(*c.take("tp_got"))
                if not is_v:
                    pe.wait_ge(*c.take(f"crow{slot}", 32))
                for gg in range(NKV):
                    for pg in range(2):
                        last = tr(ptr[:, (gg * 2 + pg) * P:(gg * 2 + pg + 1) * P],
                                  crow[:, slot, pg, is_v * CH + gg * P:is_v * CH + (gg + 1) * P], ident)
                last.then_inc(*c.give("tp_put"))
                if is_v:
                    pe.wait_ge(*c.same("tp_put"))
                    pe.sem_inc(*c.give("crow_used"))

            def hidden_part(t):
                i, j0 = t // 8, t % 8 * 4
                if t % 2 == 0:
                    pe.wait_ge(*c.take(f"w1_in{t // 2 % 2}", 16))
                if t == 8:
                    pe.wait_ge(*c.take("cmp_h"))
                for j in range(j0, j0 + 4):
                    last = mm(pSs[:, 0:17 * NBLK], w1s[:, j % 16, :], past[i][:, :, j:j + 225:STRIDE],
                              start=(j == 0), stop=(j == CMP_LEN - 1))
                if t % 8 == 7:
                    last.then_inc(*c.give("cmp_put"))
                    pe.wait_ge(*c.same("cmp_put"))
                    pe.sem_inc(*c.give("w1_used"))
                elif t % 2:
                    last.then_inc(*c.give("w1_used"))

            def sum_squares(ready):
                pe.wait_ge(*c.take(ready))
                pe.wait_ge(*c.take("misc_got"))
                mm(pmisc[:, 0:T], ones[:, :], acc[:, :], start=True, stop=True).then_inc(*c.give("misc_put"))

            def kv_turn(j):
                is_v = (j % 4) // 2
                pe.wait_ge(*c.take("v_ready" if is_v else "kv_done"))
                if j:
                    pe.wait_ge(*c.take("tp_got"))
                src = vtmp[:, j % 2, :] if (j >= 4 and is_v) else kvT[:, (0, 4, 6)[j // 4] + (j % 4), :]
                for i in range(2):
                    tr(ptr[:, i * P:(i + 1) * P], src[:, i * P:(i + 1) * P], ident)
                tr(ptr[0:NTS, SEQ:SEQ + P], src[:, SEQ:T], ident).then_inc(*c.give("tp_put"))

            def pe_before(s, g):
                if s == 0:
                    pe.wait_ge(*c.take("v_turn"))
                    mm(ptr[0:NBLK, 0:P], avc[:, 4 * NBLK:5 * NBLK], w2[:, 1, :], start=True, stop=True).then_inc(
                        *c.give("tp_put"))
                    pe.wait_ge(*c.take("tp_got"))
                if s in KTURN:
                    k_turn(s, 0)

            def k_turn(s, b):
                slot = 2 * (KTURN[s][1]) + b
                pe.wait_ge(*c.take(f"cache{slot}", 32))
                for gg in range(NKV):
                    for pg in range(2):
                        last = tr(ptr[:, (gg * 2 + pg) * P:(gg * 2 + pg + 1) * P], ring[:, slot, pg, gg * P:(gg + 1) * P], ident)
                last.then_inc(*c.give("tp_put"))

            def pe_tasks(s, g):
                if s - 2 in PROMPT:
                    head, kind = PROMPT[s - 2]
                    pe.wait_ge(*c.take("pt_got"))
                    if kind < 2:
                        if kind == 0:
                            pe.wait_ge(*c.take("op_got"))
                        mm(pO[:, 0:SEQ], vcur[:, kind, 0, :], probT[:, 0:SEQ], start=(kind == 0), stop=False, skip_group_check=True)
                        mm(pO[:, P:SEQ], vcur[:, kind, 1, :], probT[:, SEQ:3 * P], start=False, stop=False, skip_group_check=True)
                    else:
                        mm(pO[:, 0:SEQ], vcp[:, :], probT[0:NBLK, 0:SEQ], start=False, stop=True,
                           skip_group_check=True).then_inc(*c.give("op_put"))
                if s in PROMPT:
                    head, kind = PROMPT[s]
                    if kind == 0:
                        pe.wait_ge(*c.take("qc_ready"))
                    pe.wait_ge(*c.take("sp_e"))
                    q = qc[:, head % 2, :]
                    if kind < 2:
                        mm(pS[:, 0:P], q[:, 0:P], kvT[:, bass.ds(g + (4 + 2 * kind), 1), 0:P].rearrange("p a t -> p (a t)"), start=True, stop=True)
                        mm(pS[:, P:3 * P], q[:, P:SEQ], kvT[:, bass.ds(g + (4 + 2 * kind), 1), 0:SEQ].rearrange("p a t -> p (a t)"), start=True,
                           stop=True).then_inc(*c.give("sp_put"))
                    else:
                        kc = kcT[:, bass.ds(g * NBLK + NSEQ * NBLK, NBLK)]
                        mm(pS[:, 0:NBLK], q[:, 0:P], kc, start=True, stop=True)
                        mm(pS[:, NBLK:2 * NBLK], q[:, P:SEQ], kc, start=True, stop=True).then_inc(*c.give("sp_put"))
                if s - 1 in PROMPT:
                    head, kind = PROMPT[s - 1]
                    pr = prob[:, (s - 1) % 2, :]
                    pe.wait_ge(*c.take("sp_p"))
                    if kind < 2:
                        for i in range(3):
                            last = tr(pPT[:, i * P:(i + 1) * P], pr[:, i * P:(i + 1) * P], ident)
                    else:
                        for i in range(2):
                            last = tr(pPT[0:NBLK, i * P:(i + 1) * P], pr[:, i * NBLK:(i + 1) * NBLK], ident)
                    last.then_inc(*c.give("pt_put"))
                if s in KTURN:
                    pe.wait_ge(*c.take("tp_got"))
                    k_turn(s, 1)
                if s in VTURN:
                    pe.wait_ge(*c.take("av_ready"))
                    for q in range(4):
                        last = mm(ptr[0:NBLK, q * P:(q + 1) * P], avc[:, q * NBLK:(q + 1) * NBLK], w2[:, 1, :], start=True, stop=True)
                    last.then_inc(*c.give("tp_put"))
                if s - 3 in SAMPLE:
                    pp, kind = SAMPLE[s - 3]
                    pe.wait_ge(*c.take("pts_got"))
                    if kind == 0:
                        pe.wait_ge(*c.take("os_got"))
                    for q in range(4):
                        b, gg = q // 2, q % 2
                        o = pOs[:, q * 16:(q + 1) * 16]
                        if kind < 2:
                            for pg in range(2):
                                mm(o, ring[:, 2 * kind + b, pg, CH // 1 + gg * P:CH + (gg + 1) * P],
                                   sprobT[:, pg * P + q * 32:pg * P + q * 32 + 16], start=(kind == 0 and q == 0 and pg == 0),
                                   stop=False, skip_group_check=True)
                            last = mm(o, vtok[0:NTS, kind, 2, gg * P:(gg + 1) * P], sprobT[0:NTS, SEQ + q * 32:SEQ + q * 32 + 16],
                                      start=False, stop=False, skip_group_check=True)
                        else:
                            last = mm(o, vcs[:, q, :], sprobT[0:NBLK, q * 32:q * 32 + 16], start=False, stop=(q == 3),
                                      skip_group_check=True)
                    last.then_inc(*c.give("cache_used" if kind < 2 else "os_put"))
                if s - 1 in SAMPLE:
                    pp, kind = SAMPLE[s - 1]
                    pe.wait_ge(*c.take("tp_got"))
                    if kind == 0:
                        pe.wait_ge(*c.take("qs_ready"))
                    for q in range(4):
                        o = pSs[q * 32:(q + 1) * 32, :]
                        if kind < 2:
                            mm(o[:, 0:SEQ], qs[:, q, :], kwork[:, q, :], start=True, stop=True)
                            last = mm(o[:, SEQ:T], qs[:, q, :], kvT[:, 4 + 2 * kind + q % 2, SEQ:T], start=True, stop=True)
                        else:
                            last = mm(o[:, 0:NBLK], qs[:, q, :], avc[:, (5 + q) * NBLK:(6 + q) * NBLK], start=True, stop=True)
                    last.then_inc(*c.give("ss_put"))
                if s - 2 in SAMPLE:
                    pp, kind = SAMPLE[s - 2]
                    pe.wait_ge(*c.take("ss_p"))
                    if kind < 2:
                        for i in range(2):
                            tr(pSs[:, i * P:(i + 1) * P], sprob[:, i * P:(i + 1) * P], ident)
                        last = tr(pSs[0:NTS, SEQ:SEQ + P], sprob[:, SEQ:T], ident)
                    else:
                        last = tr(pSs[0:NBLK, 0:P], sprob[:, 0:NBLK], ident)
                    last.then_inc(*c.give("pts_put"))

            with Loop(pe, c, "layer", DEPTH) as l:
                pe.wait_ge(*c.take("vec_in", 128))
                pe.wait_ge(*c.take("misc_got"))
                tr(pmisc[:, 0:120], stage[0:120, 0, 0:P], ident[0:120, 0:120])
                tr(pmisc[:, 128:192], stage[0:64, 1, 0:P], ident[0:64, 0:64])
                for k in range(8):
                    last = tr(pmisc[:, 192 + k * 16:208 + k * 16], xsrow[:, k * P:(k + 1) * P], ident[0:16, 0:16])
                last.then_inc(*c.give("misc_put"))
                for s in range(2):
                    pe.wait_ge(*c.ahead(f"bank{s}"))
                with Loop(pe, c, "shift", 4):
                    mod_tiles(past_turn)
                    pe.wait_ge(*c.take("tp_got"))
                for q in range(4):
                    mod_tiles(lambda j: hidden_part(4 * q + j))
                sum_squares("ssq_ready")
                with Loop(pe, c, "ada2", 4):
                    mod_tiles()
                pe.wait_ge(*c.take("h_ready", 4))
                with Loop(pe, c, "q", 2):
                    for s in range(4):
                        tile(s % 2)
                for j in range(12):
                    tile(j % 2)
                    if j:
                        kv_turn(j - 1)
                tile(0, NG)
                kv_turn(11)
                pe.wait_ge(*c.take("tp_got"))
                pe.wait_ge(*c.take("gate_ready"))
                pe.wait_ge(*c.take("misc_got"))
                apart(pe)
                for i in range(2):
                    tr(pmisc[:, i * NG:(i + 1) * NG], cbuf[0:NG, 0, i * P:(i + 1) * P], ident[0:NG, 0:NG])
                gx = ubuf[0:NG, :, :].rearrange("p a b -> p (a b)")
                for p in range(4):
                    last = tr(pmisc[:, 48 + p * NG:48 + (p + 1) * NG], gx[:, p * P:(p + 1) * P], ident[0:NG, 0:NG])
                last.then_inc(*c.give("misc_put"))
                pe.wait_ge(*c.take("raw0", 16 * 21))
                pe.wait_ge(*c.take("raw1", 16 * 21))
                pe.wait_ge(*c.take("cmp_h"))
                for i in range(2):
                    for j in range(CMP_LEN):
                        at = 2 * i * T + j
                        last = mm((pSs, pPT)[i][0:NROW, 0:P], kvf[:, at:at + (NROW - 1) * STRIDE + 1:STRIDE], w1v[i][:, j, :],
                                  start=(j == 0), stop=(j == CMP_LEN - 1))
                    last.then_inc(*c.give("cmp_put"))
                for i in range(2):
                    pe.wait_ge(*c.take("cmp_row"))
                    apart(pe)
                    tr((pSs, pPT)[i][:, 256:256 + NROW], gz[0:NROW, 1, i * P:(i + 1) * P], ident[0:NROW, 0:NROW]).then_inc(
                        *c.give("cmp_put"))
                c.skip("lo_ready", 4)
                c.skip("raw0", 16 * 14)
                c.skip("raw1", 16 * 14)
                pe.wait_ge(*c.take("cmp_h", 2))
                pe.wait_ge(*c.take("cmp_a"))
                mm(pSs[:, 0:(NSEQ + 2) * NBLK], w2[:, 0, :], cact[:, 0, :], start=True, stop=True).then_inc(*c.give("kc_put"))
                pe.wait_ge(*c.take("kc_got"))

                with Loop(pe, c, "turn", 2) as g:
                    for s in range(16):
                        pe_before(s, g)
                        tile(s % 2)
                        pe_tasks(s, g)
                sum_squares("a_done")
                with Loop(pe, c, "z", 2):
                    for s in range(4):
                        tile(s % 2)
                pe.wait_ge(*c.take("u_put"))
                for half in range(2):
                    for k in range(4):
                        last = tr(ptr[0:2 + 2 * NB, k * P:(k + 1) * P], uo[:, half * 4 + k, :], ident)
                    last.then_inc(*c.give("tp_put"))
                    pe.wait_ge(*c.take("tp_got"))
                sum_squares("b_done")
                pe.wait_ge(*c.take("y_hl", 4))
                with Loop(pe, c, "out", 4):
                    for s in range(4):
                        tile(s % 2)
                sum_squares("y_done")
            pe.wait_ge(*c.take("ssq_ready"))
            for k in range(KT):
                b = k % 2
                pe.wait_ge(*c.take(f"bank{b}"))
                for i in range(2):
                    tr(proj[b][:, i * P:(i + 1) * P], xv[:, k, i * P:(i + 1) * P], ident)
                tr(proj[b][0:NTS, SEQ:SEQ + P], xv[:, k, SEQ:T], ident).then_inc(*c.give("fin_put"))

        @block.scalar
        def _(act):
            c = Counts(act, sems, per.setdefault("act", {}))
            fn = nc.scalar.activation

            def copy(out, in_, scale=1.0):
                return fn(out, in_, ACT.Copy, scale=scale)

            def split(k):
                if k % 2 == 0:
                    act.wait_ge(*c.take(f"raw{k // 2 % 2}", 16))
                copy(w_hi[:, k % 2, :, :], rawv[k // 2 % 2][:, :, (k % 2) * P:(k % 2 + 1) * P]).then_inc(*c.give("hi_ready"))

            def rstd(n=DM):
                act.wait_ge(*c.take("misc_put"))
                fn(rs[:, :], pmisc[:, 0:T], ACT.Sqrt, scale=1.0 / n, bias=eps).then_inc(*c.give("misc_got"))

            act.wait_ge(*c.take("c_in", 32))
            fn(mixf[0:ROWS, 0:DM], raw[0:ROWS, 1, DM:2 * DM], ACT.Tanh, scale=0.5).then_inc(*c.give("c_tanh"))
            act.wait_ge(*c.take("mem_set"))
            act.sem_inc(*c.give("sp_e"))
            c.skip("misc_put")
            c.skip("misc_got", 2)
            c.skip("bank0", 1 + KT // 2)
            c.skip("bank1", 1 + KT // 2)

            def mod_slots():
                c.skip("misc_put")
                for k in range(4):
                    yield k
                    act.wait_ge(*c.take("tile_done"))
                    copy(mrow[:, k % 2, :], proj[k % 2][0:2 * ROWS, 0:P]).then_inc(*c.give("mod_row"))
                c.skip("misc_got")

            def past_turned(i, j):
                act.wait_ge(*c.take("tp_put"))
                copy(past[j % 2][:, bass.ds(i * 4 + j // 2 * 2, 2), :], ptr[:, :].rearrange("p (g t) -> p g t", g=2)).then_inc(
                    *c.give("tp_got"))

            def turn_out(j, l):
                br, is_v, gg = j // 4, j % 4 // 2, j % 2
                keep = is_v and br
                dst = vtok[:, br - 1, :, :] if keep else stage[:, :, :]
                if not gg and j:
                    act.wait_ge(*c.same("stored"))
                act.wait_ge(*c.take("tp_put"))
                copy(dst[:, 0:2, gg * P:(gg + 1) * P], ptr[:, 0:SEQ].rearrange("p (i d) -> p i d", i=2)).then_inc(*c.give("act_step"))
                copy(dst[0:NTS, 2, gg * P:(gg + 1) * P], ptr[0:NTS, SEQ:SEQ + P]).then_inc(*c.give("tp_got"))
                if gg:
                    act.wait_ge(*c.same("act_step"))
                    act.wait_ge(*c.same("tp_got"))
                    o_p, o_s, n = (kv_p, kv_s, br * 2 + is_v) if br < 2 else (win_p, win_s, is_v)
                    act.dma_start(o_p[bass.ds(l, 1), 0, :, n].rearrange("l (i p) g d -> p (l i) (g d)", p=P),
                                  dst[:, 0:2, :]).then_inc(*c.give("stored", 16))
                    if br < 2:
                        act.dma_start(o_s[bass.ds(l, 1), :, :, n].rearrange("l b t g d -> (l b t) (g d)"),
                                      dst[0:NTS, 2, :]).then_inc(*c.give("stored", 16))
                    else:
                        act.dma_start(o_s[bass.ds(l, 1), :, SEQ - TS:SEQ, n].rearrange("l b t g d -> (l b) t (g d)"),
                                      dst[0:NTS, 2, :]).then_inc(*c.give("stored", 16))

            with Loop(act, c, "layer", DEPTH) as l:
                c.skip("misc_put")
                c.skip("misc_got")
                split(0)
                act.wait_ge(*c.take("x_tile", KT))
                with Loop(act, c, "shift", 4) as i:
                    for k in mod_slots():
                        split((k + 1) % 4)
                        if k:
                            past_turned(i, k - 1)
                    past_turned(i, 3)
                for q in range(4):
                    for k in mod_slots():
                        split((k + 1) % 4)
                    if q % 2:
                        act.wait_ge(*c.take("cmp_h"))
                        fn(gz[:, 0, 0:NSEQ * NBLK], cbuf[:, 1, 0:NSEQ * NBLK], ACT.Tanh, scale=0.5).then_inc(*c.give("cmp_tanh"))
                rstd()
                with Loop(act, c, "ada2", 4) as i:
                    for k in mod_slots():
                        split((k + 1) % 4)
                        if k == 0:
                            act.wait_ge(*c.take("xn"))
                            for kk in range(4):
                                t = i * 4 + kk
                                fn(mix[:, bass.ds(t, 1), 0:SEQ].rearrange("p a t -> p (a t)"),
                                   mix[:, bass.ds(t, 1), 0:SEQ].rearrange("p a t -> p (a t)"), ACT.Identity,
                                   scale=mod[:, bass.ds(t + 16, 1), 0], bias=mod[:, bass.ds(t, 1), 0]).then_inc(*c.give("act_step"))
                            act.wait_ge(*c.same("act_step"))
                            act.wait_ge(*c.take("h_s"))
                            copy(h_hi[:, bass.ds(i * 4, 4), :], mix[:, bass.ds(i * 4, 4), :]).then_inc(*c.give("h_hi"))
                with Loop(act, c, "q", 2):
                    for k in range(4):
                        split((k + 1) % 4)
                        act.wait_ge(*c.take("tile_done"))
                        c.skip(f"bank{k % 2}")
                for j in range(12):
                    if j < 11:
                        split((j + 1) % 4)
                    else:
                        act.wait_ge(*c.take("graw", 16))
                        copy(w_hi[:, 0, :, 0:NG], graw).then_inc(*c.give("hi_ready"))
                    act.wait_ge(*c.take("tile_done"))
                    if j % 4 < 2:
                        c.skip(f"bank{j % 2}")
                    else:
                        dst = kvT[:, 2 + j % 2, :] if j < 4 else vtmp[:, j % 2, :]
                        copy(dst, proj[j % 2][:, 0:T]).then_inc(*c.give("v_ready"))
                        act.wait_ge(*c.same("v_ready"))
                        act.sem_inc(*c.give(f"bank{j % 2}"))
                    if j:
                        turn_out(j - 1, l)
                act.wait_ge(*c.take("tile_done"))
                fn(cbuf[0:NG, 0, :], proj[0][0:NG, 0:T], ACT.Tanh, scale=0.5).then_inc(*c.give("bank0"))
                turn_out(11, l)
                c.skip("misc_put")
                c.skip("misc_got")
                c.skip("raw0", 64)
                c.skip("raw1", 64)
                for i in range(2):
                    act.wait_ge(*c.take("cmp_h"))
                    fn(gz[:, 0, 0:2 * NBLK], cbuf[:, 1, 0:2 * NBLK], ACT.Tanh, scale=0.5).then_inc(*c.give("cmp_tanh"))
                split(0)
                with Loop(act, c, "turn", 2) as g:
                    for s in range(16):
                        if s == 0:
                            act.wait_ge(*c.take("tp_put"))
                            copy(vcp[:, :], ptr[0:NBLK, 0:P], scale=0.5).then_inc(*c.give("tp_got"))
                        if s in KTURN:
                            act.wait_ge(*c.take("tp_put"))
                            copy(kwork[:, 0:2, :], ptr[:, :].rearrange("p (g t) -> p g t", g=2)).then_inc(*c.give("tp_got"))
                        split((s + 1) % 4)
                        act.wait_ge(*c.take("tile_done"))
                        kind, ti = s // 2 % 4, s % 2
                        if kind == 0:
                            copy(cbuf[:, ti, :], proj[ti][:, 0:T]).then_inc(*c.give(f"bank{ti}"))
                        else:
                            c.skip(f"bank{ti}")
                        if kind == 2:
                            fn(gz[:, ti, :], proj[ti][:, 0:T], ACT.Tanh, scale=0.5).then_inc(*c.give("z_t"))
                        if s in PROMPT:
                            knd = PROMPT[s][1]
                            act.wait_ge(*c.take("sp_nm"))
                            for i in range(2):
                                w = (slice(0, P), slice(P, 3 * P))[i] if knd < 2 else slice(i * NBLK, (i + 1) * NBLK)
                                fn(prob[:, s % 2, w], pS[:, w], ACT.Exp, scale=SCALE, bias=small[:, i:i + 1],
                                   accum_out=small[:, 2 + i:3 + i]).then_inc(*c.give(("act_step", "sp_e")[i]))
                        if s - 1 in PROMPT:
                            act.wait_ge(*c.take("pt_put"))
                            w = (slice(0, P), slice(0, 3 * P)) if PROMPT[s - 1][1] < 2 else (slice(0, NBLK), slice(0, SEQ))
                            copy(probT[w], pPT[w]).then_inc(*c.give("pt_got"))
                        if s in KTURN:
                            act.wait_ge(*c.take("tp_put"))
                            copy(kwork[:, 2:4, :], ptr[:, :].rearrange("p (g t) -> p g t", g=2)).then_inc(*c.give("tp_got"))
                        if s in VTURN:
                            act.wait_ge(*c.take("tp_put"))
                            copy(vcs[:, :, :], ptr[0:NBLK, :].rearrange("p (q d) -> p q d", q=4), scale=0.5).then_inc(*c.give("tp_got"))
                        if s - 1 in SAMPLE:
                            w = T if SAMPLE[s - 1][1] < 2 else NBLK
                            act.wait_ge(*c.take("ss_nm"))
                            fn(sprob[:, 0:w], pSs[:, 0:w], ACT.Exp, scale=SCALE, bias=small[:, 4:5],
                               accum_out=small[:, 5:6]).then_inc(*c.give("ss_e"))
                        if s - 2 in SAMPLE:
                            act.wait_ge(*c.take("pts_put"))
                            if SAMPLE[s - 2][1] < 2:
                                copy(sprobT[:, 0:SEQ], pSs[:, 0:SEQ]).then_inc(*c.give("act_step"))
                                copy(sprobT[0:NTS, SEQ:3 * P], pSs[0:NTS, SEQ:3 * P]).then_inc(*c.give("act_step"))
                                act.wait_ge(*c.same("act_step"))
                                act.sem_inc(*c.give("pts_got"))
                            else:
                                copy(sprobT[0:NBLK, 0:P], pSs[0:NBLK, 0:P]).then_inc(*c.give("pts_got"))
                rstd(NC_CONV)
                with Loop(act, c, "z", 2):
                    for k in range(4):
                        split((k + 1) % 4)
                        act.wait_ge(*c.take("tile_done"))
                        fn(gz[:, k % 2, :], proj[k % 2][:, 0:T], ACT.Tanh, scale=0.5).then_inc(*c.give("z_t"))
                        c.skip(f"bank{k % 2}")
                for half in range(2):
                    act.wait_ge(*c.take("tp_put"))
                    copy(uorow[:, half * 512:(half + 1) * 512], ptr[0:2 + 2 * NB, :]).then_inc(*c.give("tp_got"))
                act.wait_ge(*c.same("tp_got"))
                act.dma_start(conv_p[bass.ds(l, 1), 0].rearrange("l i n -> (l i) n"), uorow[0:2, :]).then_inc(*c.give("stored", 16))
                act.dma_start(conv_s[bass.ds(l, 1)].rearrange("l b i n -> (l b i) n"), uorow[2:2 + 2 * NB, :]).then_inc(
                    *c.give("stored", 16))
                rstd(NC_CONV)
                act.wait_ge(*c.same("stored"))
                for i in range(4):
                    act.wait_ge(*c.take("y_f"))
                    copy(h_hi[:, 4 * i:4 * i + 4, :], mix[:, 4 * i:4 * i + 4, :]).then_inc(*c.give("y_hi"))

                def out_slot(k, t, ahead):
                    if ahead:
                        split((k + 1) % 4)
                    act.wait_ge(*c.take("tile_done"))
                    act.wait_ge(*c.take("sq_free"))
                    fn(gz[:, k % 2, :], proj[k % 2][:, 0:T], ACT.Square).then_inc(*c.give("y_sq"))
                    copy(mix[:, t, :], proj[k % 2][:, 0:T].unsqueeze(1)).then_inc(*c.give(f"bank{k % 2}"))

                with Loop(act, c, "out", 3) as i:
                    for k in range(4):
                        out_slot(k, bass.ds(i * 4 + k, 1), True)
                for k in range(4):
                    out_slot(k, slice(12 + k, 13 + k), k < 3)
                rstd()
            for k in range(KT):
                b = k % 2
                act.wait_ge(*c.take("fin_put"))
                copy(raw[:, 0, :].rearrange("p (i n) -> p i n", i=2)[:, :, k * P:(k + 1) * P],
                     proj[b][:, 0:SEQ].rearrange("p (i n) -> p i n", i=2)).then_inc(*c.give("act_step"))
                copy(raw[0:NTS, 1, k * P:(k + 1) * P], proj[b][0:NTS, SEQ:SEQ + P]).then_inc(*c.give(f"bank{b}"))
            act.wait_ge(*c.same("act_step"))
            act.wait_ge(*c.same("bank0"))
            act.wait_ge(*c.same("bank1"))
            for i in range(2):
                act.dma_start(y_p[0, i * P:(i + 1) * P, :], raw[:, 0, i * DM:(i + 1) * DM]).then_inc(*c.give("stored", 16))
            act.dma_start(y_s.rearrange("b t d -> (b t) d"), raw[0:NTS, 1, 0:DM]).then_inc(*c.give("stored", 16))
            act.wait_ge(*c.same("stored"))

        @block.vector
        def _(dve):
            c = Counts(dve, sems, per.setdefault("dve", {}))
            tt, ts, stt, cp = nc.vector.tensor_tensor, nc.vector.tensor_scalar, nc.vector.scalar_tensor_tensor, nc.vector.tensor_copy

            def link(ins):
                ins.then_inc(*c.give("dve_step"))
                dve.wait_ge(*c.same("dve_step"))

            nc.vector.memset(ones[:, :], 1.0).then_inc(*c.give("bank0"))
            for i in range(2):
                nc.vector.memset(past[i][:, 16, :], 0.0).then_inc(*c.give("dve_step" if i else "bank1"))
            nc.vector.memset(eps, EPS).then_inc(*c.give("misc_got"))
            nc.vector.memset(qs[:, :, :], 0.0).then_inc(*c.give("dve_step"))
            nc.vector.memset(small[:, 0:15], 0.0).then_inc(*c.give("mem_set"))
            for k in range(KT):
                dve.wait_ge(*c.take("x_put"))
                cp(xv[:, k, :], proj[k % 2][:, 0:T]).then_inc(*c.give(f"bank{k % 2}"))
            dve.wait_ge(*c.take("c_tanh"))
            stt(mixf[0:ROWS, 0:DM], mixf[0:ROWS, 0:DM], 1.0, raw[0:ROWS, 1, DM:2 * DM], ALU.add, ALU.mult).then_inc(*c.give("c_done"))
            dve.wait_ge(*c.take("misc_put"))
            cF = gz[:, 0, 0:KT * ROWS].rearrange("p (k r) -> p k r", k=KT)
            ts(cF, pmisc[:, 0:KT * ROWS].rearrange("p (k r) -> p k r", k=KT), 0.5, None, ALU.mult).then_inc(*c.give("misc_got"))
            dve.wait_ge(*c.same("misc_got"))
            link(cp(cHL[:, :, 0:ROWS], cF))
            tt(cHL[:, :, ROWS:2 * ROWS], cF, cHL[:, :, 0:ROWS].bitcast(F32), ALU.subtract).then_inc(*c.give("x_tile", KT))
            dve.wait_ge(*c.same("x_tile"))
            dve.sem_inc(*c.give("lo_ready", 4))
            dve.sem_inc(*c.give("op_got"))
            dve.sem_inc(*c.give("os_got"))
            c.skip("sp_e")

            def split(k, src=None):
                s, r = k % 2, rawv[k // 2 % 2][:, :, (k % 2) * P:(k % 2 + 1) * P]
                dve.wait_ge(*c.take("hi_ready"))
                tt(w_lo[:, s, :, :], r, w_hi[:, s, :, :].bitcast(F32), ALU.subtract).then_inc(*c.give("lo_ready"))

            def mod_slots(i, base):
                for k in range(4):
                    yield k
                    dve.wait_ge(*c.take("tile_done"))
                dve.wait_ge(*c.take("misc_put"))
                j = i * 4 + base
                tt(mod[:, bass.ds(j, 4), :], pmisc[:, 0:4 * ROWS].rearrange("p (k r) -> p k r", k=4),
                   vec[:, bass.ds(j, 4)].unsqueeze(2).to_broadcast([P, 4, ROWS]), ALU.add).then_inc(*c.give("misc_got"))

            def invert_rs():
                dve.wait_ge(*c.take("misc_got"))
                link(nc.vector.reciprocal(rs[:, :], rs[:, :]))

            def rope(src, dst):
                half = HD // 2
                t = ubuf[:, 0, 0:T]
                tt(t[half:P], src[0:half], cst[0:half, C_SIN:C_SIN + T], ALU.mult).then_inc(*c.give("dve_step"))
                tt(t[0:half], src[half:P], cst[half:P, C_SIN:C_SIN + T], ALU.mult).then_inc(*c.give("dve_step"))
                link(tt(dst, src, cst[:, C_COS:C_COS + T], ALU.mult))
                return tt(dst, dst, t, ALU.add)

            def one(ap):
                return ap.rearrange("p a t -> p (a t)")

            samp = lambda ap: ap.rearrange("p k (b t) -> p k b t", t=TS)

            def low(i):
                dve.wait_ge(*c.take("y_hi"))
                tt(h_lo[:, 4 * i:4 * i + 4, :], mix[:, 4 * i:4 * i + 4, :], h_hi[:, 4 * i:4 * i + 4, :].bitcast(F32),
                   ALU.subtract).then_inc(*c.give("y_hl"))

            def conv_slot(s, g):
                kind, ti = s // 2 % 4, s % 2
                out, bank = proj[ti][:, 0:T], f"bank{ti}"
                u = ubuf[:, ti, :]
                us = u[:, 2 + SEQ:].rearrange("p (b t) -> p b t", b=NB)
                cs = cbuf[:, ti, SEQ:T].rearrange("p (b t) -> p b t", b=NB)
                tile = 2 * (s // 8) + ti
                if kind == 0:
                    c.skip(bank)
                elif kind == 1:
                    tt(u[:, 2:2 + SEQ], out[:, 0:SEQ], cbuf[:, ti, 0:SEQ], ALU.mult).then_inc(*c.give("dve_step"))
                    cp(us[:, :, 0:2], one(stT[:, bass.ds(g * 4 + tile, 1), :]).rearrange("p (b i) -> p b i", b=NB)).then_inc(
                        *c.give("dve_step"))
                    tt(us[:, :, 2:], out[:, SEQ:T].rearrange("p (b t) -> p b t", b=NB), cs, ALU.mult).then_inc(*c.give(bank))
                    dve.wait_ge(*c.same("dve_step"))
                    dve.wait_ge(*c.same(bank))
                    un = one(uo[:, bass.ds(g * 4 + tile, 1), :])
                    cp(un[:, 0:2], u[:, SEQ:SEQ + 2]).then_inc(*c.give("dve_step"))
                    cp(un[:, 2:].rearrange("p (b i) -> p b i", b=NB), us[:, :, TS:]).then_inc(*c.give("dve_step"))
                    for i in range(3):
                        w = vec[:, bass.ds(g * 4 + (96 + 8 * i + tile), 1)]
                        if i == 0:
                            ts(cbuf[:, ti, 0:SEQ], u[:, 0:SEQ], w, None, ALU.mult).then_inc(*c.give("dve_step"))
                            link(ts(cs, us[:, :, 0:TS], w, None, ALU.mult))
                        else:
                            stt(cbuf[:, ti, 0:SEQ], u[:, i:i + SEQ], w, cbuf[:, ti, 0:SEQ], ALU.mult, ALU.add).then_inc(
                                *c.give("dve_step"))
                            link(stt(cs, us[:, :, i:i + TS], w, cs, ALU.mult, ALU.add))
                elif kind == 2:
                    dve.wait_ge(*c.take("z_t"))
                    stt(gz[:, ti, :], gz[:, ti, :], 1.0, out, ALU.add, ALU.mult).then_inc(*c.give(bank))
                else:
                    ya = one(mix[:, bass.ds(g * 4 + tile, 1), :])
                    stt(ya, out, 0.5, cbuf[:, ti, :], ALU.mult, ALU.mult).then_inc(*c.give(bank))
                    dve.wait_ge(*c.same(bank))
                    tt(ya, ya, gz[:, ti, :], ALU.mult).then_inc(*c.give("ya_ready"))

            def hidden(i, n, dst, at=0):
                dve.wait_ge(*c.take("cmp_put"))
                if at == 0:
                    link(cp(small[:, 12 + i:13 + i], pSs[:, (NSEQ * NBLK + 2 * i):(NSEQ * NBLK + 2 * i + 1)]))
                src, got = pSs[:, 0:n], cbuf[:, 1, 0:n]
                if at:
                    src = (pSs, pPT)[i][:, at:at + 2 * T // STRIDE].rearrange("p (g n) -> p g n", g=2)[:, :, 0:NBLK]
                    got = got.rearrange("p (g n) -> p g n", g=2)
                ts(got, src, small[:, 12 + i:13 + i], None, ALU.add).then_inc(*c.give("cmp_h"))
                dve.wait_ge(*c.take("cmp_tanh"))
                link(stt(dst, gz[:, 0, 0:n], 1.0, cbuf[:, 1, 0:n], ALU.add, ALU.mult))

            with Loop(dve, c, "layer", DEPTH) as l:
                dve.wait_ge(*c.take("misc_put"))
                link(cp(vec[:, :], pmisc[:, 0:120]))
                for i in range(2):
                    link(cp(past[i][:, 16, 0:64], pmisc[:, 128:192]))
                cp(stT[:, :, :], pmisc[:, 192:320].rearrange("p (k r) -> p k r", k=8)).then_inc(*c.give("misc_got"))
                split(0)
                with Loop(dve, c, "shift", 4) as i:
                    for k in mod_slots(i, 0):
                        split((k + 1) % 4)
                for q in range(4):
                    for k in mod_slots(0, 16 + 4 * q):
                        split((k + 1) % 4)
                    if q % 2:
                        hidden(q // 2, NSEQ * NBLK, cact[:, q // 2, 0:NSEQ * NBLK])
                dve.wait_ge(*c.same("misc_got"))
                c.skip("misc_put")
                link(stt(mod[:, 16:32, :], mod[:, 16:32, :], 1.0, vec[:, 48:64].unsqueeze(2).to_broadcast([P, 16, ROWS]),
                         ALU.add, ALU.mult))
                invert_rs()
                with Loop(dve, c, "ada2", 4) as i:
                    for k in mod_slots(i, 32):
                        if k == 0:
                            m4 = mix[:, bass.ds(i * 4, 4), :]
                            tt(m4, xv[:, bass.ds(i * 4, 4), :], rs[:, :].unsqueeze(1).to_broadcast([P, 4, T]),
                               ALU.mult).then_inc(*c.give("xn"))
                            dve.wait_ge(*c.same("xn"))
                            m4s = samp(mix[:, bass.ds(i * 4, 4), SEQ:T])
                            link(tt(m4s, m4s, mod[:, bass.ds(i * 4 + 16, 4), 1:ROWS].unsqueeze(3).to_broadcast([P, 4, NB, TS]), ALU.mult))
                            tt(m4s, m4s, mod[:, bass.ds(i * 4, 4), 1:ROWS].unsqueeze(3).to_broadcast([P, 4, NB, TS]),
                               ALU.add).then_inc(*c.give("h_s"))
                        split((k + 1) % 4)
                        if k == 1:
                            dve.wait_ge(*c.take("h_hi"))
                            tt(h_lo[:, bass.ds(i * 4, 4), :], mix[:, bass.ds(i * 4, 4), :],
                               h_hi[:, bass.ds(i * 4, 4), :].bitcast(F32), ALU.subtract).then_inc(*c.give("h_ready"))
                dve.wait_ge(*c.same("misc_got"))
                link(tt(mod[:, 32:48, :], mod[:, 32:48, :], vec[:, 80:96].unsqueeze(2).to_broadcast([P, 16, ROWS]), ALU.mult))
                with Loop(dve, c, "q", 2) as i:
                    for k in range(4):
                        split((k + 1) % 4)
                        dve.wait_ge(*c.take("tile_done"))
                        rope(proj[k % 2][:, 0:T], one(mix[:, bass.ds(i * 4 + (8 + k), 1), :])).then_inc(*c.give(f"bank{k % 2}"))
                        dve.wait_ge(*c.same(f"bank{k % 2}"))
                for j in range(12):
                    if j < 11:
                        split((j + 1) % 4)
                    else:
                        dve.wait_ge(*c.take("hi_ready"))
                        tt(w_lo[:, 0, :, 0:NG], graw, w_hi[:, 0, :, 0:NG].bitcast(F32), ALU.subtract).then_inc(*c.give("lo_ready"))
                    dve.wait_ge(*c.take("tile_done"))
                    if j % 4 < 2:
                        rope(proj[j % 2][:, 0:T], kvT[:, (0, 4, 6)[j // 4] + j % 4, :]).then_inc(*c.give("kv_done"))
                        dve.wait_ge(*c.same("kv_done"))
                        dve.sem_inc(*c.give(f"bank{j % 2}"))
                    else:
                        c.skip(f"bank{j % 2}")
                dve.wait_ge(*c.take("tile_done"))
                dve.wait_ge(*c.take("bank0"))
                link(ts(cbuf[0:NG, 0, :], cbuf[0:NG, 0, :], 0.5, 0.5, ALU.mult, ALU.add))
                gx = ubuf[0:NG, :, :].rearrange("p a b -> p (a b)")
                for p in range(4):
                    last = cp(gx[:, p * P:(p + 1) * P].rearrange("p (b r t) -> p b r t", b=2, t=TS),
                              cbuf[0:NG, 0, SEQ + 8 * p:SEQ + 8 * p + 8].rearrange("p (b t) -> p b t", b=2).unsqueeze(2).to_broadcast(
                                  [NG, 2, 16, TS])).then_inc(*c.give("dve_step" if p < 3 else "gate_ready"))
                dve.wait_ge(*c.take("misc_put"))
                cp(gtok[:, :, :], pmisc[:, 0:2 * NG].rearrange("p (i n) -> p i n", i=2)).then_inc(*c.give("dve_step"))
                gm = ubuf[:, 0, 0:4 * NG]
                tt(gm.rearrange("p (q n) -> p q n", q=4), pmisc[:, 48:48 + 4 * NG].rearrange("p (q n) -> p q n", q=4),
                   cst[:, C_GM:C_GM + NG].unsqueeze(1).to_broadcast([P, 4, NG]), ALU.mult).then_inc(*c.give("misc_got"))
                dve.wait_ge(*c.same("misc_got"))
                link(nc.vector.tensor_reduce(gsm[:, :, :], gm.rearrange("p (q h b) -> p q b h", q=4, b=3), AX_X, ALU.add))
                link(nc.vector.memset(ubuf[:, :, 0:2], 0.0))

                for i in range(2):
                    dve.wait_ge(*c.take("cmp_put"))
                    dve.sem_inc(*c.give("lo_ready", 2))
                    cp(gz[0:NROW, 1, i * P:(i + 1) * P], (pSs, pPT)[i][0:NROW, 0:P]).then_inc(*c.give("cmp_row"))
                for i in range(2):
                    hidden(i, 2 * NBLK, cact[:, i, NSEQ * NBLK:(NSEQ + 2) * NBLK], 256)
                nc.vector.memset(small[:, 14:15], 0.0).then_inc(*c.give("cmp_a"))
                dve.wait_ge(*c.take("kc_put"))
                ts(kcT[:, :], pSs[:, 0:(NSEQ + 2) * NBLK], 0.5, None, ALU.mult).then_inc(*c.give("kc_got"))
                split(0)

                with Loop(dve, c, "turn", 2) as g:
                    for s in range(16):
                        if s - 5 in (0, 3, 6, 9):
                            dve.wait_ge(*c.take("op_put"))
                            cp(one(mix[:, bass.ds(g * 4 + (8 + (s - 5) // 3), 1), 0:SEQ]), pO[:, 0:SEQ]).then_inc(*c.give("op_got"))
                        if s in (8, 15):
                            pp = int(s == 15)
                            dve.wait_ge(*c.take("os_put"))
                            for q in range(4):
                                cp(mix[:, 8 + (q % 2) * 4:12 + (q % 2) * 4, bass.ds(g * 16 + (SEQ + 8 * pp + 4 * (q // 2)), TS)],
                                   pOs[:, q * 16:(q + 1) * 16].rearrange("p (r t) -> p r t", r=4)).then_inc(
                                       *c.give("dve_step" if q < 3 else "os_got"))
                        if s - 1 in PROMPT:
                            head, kind = PROMPT[s - 1]
                            pr = prob[:, (s - 1) % 2, :]
                            dve.wait_ge(*c.take("sp_e"))
                            if kind == 2:
                                link(ts(small[:, 2:4], small[:, 2:4], 1e-30, None, ALU.max))
                            link(nc.vector.reciprocal(small[:, 6:8], small[:, 2:4]))
                            gcol = gtok[:, :, bass.ds(g * 12 + (3 * head + GATE[kind]), 1)].rearrange("p i a -> p (i a)")
                            link(tt(small[:, 6:8], small[:, 6:8], gcol, ALU.mult))
                            if kind < 2:
                                ts(pr[:, 0:P], pr[:, 0:P], small[:, 6:7], None, ALU.mult).then_inc(*c.give("dve_step"))
                                ts(pr[:, P:3 * P], pr[:, P:3 * P], small[:, 7:8], None, ALU.mult).then_inc(*c.give("sp_p"))
                            else:
                                pv = pr[:, 0:2 * NBLK].rearrange("p (i n) -> p i n", i=2)
                                tt(pv, pv, small[:, 6:8].unsqueeze(2).to_broadcast([P, 2, NBLK]), ALU.mult).then_inc(*c.give("sp_p"))
                        if s - 2 in SAMPLE:
                            pp, kind = SAMPLE[s - 2]
                            w = T if kind < 2 else NBLK
                            dve.wait_ge(*c.take("ss_e"))
                            link(nc.vector.reciprocal(small[:, 8:9], small[:, 5:6]))
                            gcol = gsm[:, bass.ds(g * 2 + pp, 1), GATE[kind]]
                            link(tt(small[:, 8:9], small[:, 8:9], gcol, ALU.mult))
                            ts(sprob[:, 0:w], sprob[:, 0:w], small[:, 8:9], None, ALU.mult).then_inc(*c.give("ss_p"))
                        split((s + 1) % 4)
                        dve.wait_ge(*c.take("tile_done"))
                        conv_slot(s, g)
                        if s in PROMPT:
                            kind = PROMPT[s][1]
                            dve.wait_ge(*c.take("sp_put"))
                            if kind < 2:
                                link(tt(pS[:, 0:P], pS[:, 0:P], tri, ALU.add))
                                link(tt(pS[:, 2 * P:3 * P], pS[:, 2 * P:3 * P], tri, ALU.add))
                                nc.vector.tensor_reduce(small[:, 9:10], pS[:, 0:P], AX_X, ALU.max).then_inc(*c.give("dve_step"))
                                link(nc.vector.tensor_reduce(small[:, 10:11], pS[:, P:3 * P], AX_X, ALU.max))
                                ts(small[:, 0:2], small[:, 9:11], -SCALE, None, ALU.mult).then_inc(*c.give("sp_nm"))
                            else:
                                link(tt(pS[:, 0:2 * NBLK], pS[:, 0:2 * NBLK], cst[:, C_CMP:C_CMP + 2 * NBLK], ALU.add))
                                link(nc.vector.tensor_reduce(small[:, 9:11], pS[:, 0:2 * NBLK].rearrange("p (i n) -> p i n", i=2),
                                                             AX_X, ALU.max))
                                ts(small[:, 0:2], small[:, 9:11], -1e29, -SCALE, ALU.max, ALU.mult).then_inc(*c.give("sp_nm"))
                        if s - 1 in SAMPLE:
                            pp, kind = SAMPLE[s - 1]
                            w = T if kind < 2 else NBLK
                            dve.wait_ge(*c.take("ss_put"))
                            if kind < 2:
                                link(tt(pSs[:, SEQ:T], pSs[:, SEQ:T], cst[:, bass.ds(g * (2 * NTS) + (C_NEW + pp * NTS), NTS)], ALU.add))
                            link(nc.vector.tensor_reduce(small[:, 11:12], pSs[:, 0:w], AX_X, ALU.max))
                            ts(small[:, 4:5], small[:, 11:12], -SCALE, None, ALU.mult).then_inc(*c.give("ss_nm"))
                nc.vector.memset(small[:, 14:15], 0.0).then_inc(*c.give("u_put"))
                dve.wait_ge(*c.same("u_put"))
                c.skip("misc_put")
                invert_rs()
                with Loop(dve, c, "z", 2) as i:
                    for k in range(4):
                        ya = one(mix[:, bass.ds(i * 4 + k, 1), :])
                        stt(ya, ya, vec[:, bass.ds(i * 4 + (64 + k), 1)], rs[:, :], ALU.mult, ALU.mult).then_inc(*c.give("dve_step"))
                        split((k + 1) % 4)
                        dve.wait_ge(*c.take("tile_done"))
                        dve.wait_ge(*c.take("z_t"))
                        stt(gz[:, k % 2, :], gz[:, k % 2, :], 1.0, proj[k % 2][:, 0:T], ALU.add, ALU.mult).then_inc(*c.give(f"bank{k % 2}"))
                        dve.wait_ge(*c.same(f"bank{k % 2}"))
                        yb = one(mix[:, bass.ds(i * 4 + (8 + k), 1), :])
                        stt(yb, yb, 0.5, gz[:, k % 2, :], ALU.mult, ALU.mult).then_inc(*c.give("yb_ready"))
                for i in range(4):
                    if i == 2:
                        c.skip("misc_put")
                        invert_rs()
                    if i >= 2:
                        for k in range(4 * i, 4 * i + 4):
                            stt(mix[:, k, :], mix[:, k, :], vec[:, 64 + k:65 + k], rs[:, :], ALU.mult, ALU.mult).then_inc(
                                *c.give("dve_step" if k < 4 * i + 3 else "y_f"))
                    else:
                        nc.vector.memset(small[:, 14:15], 0.0).then_inc(*c.give("y_f"))
                    dve.wait_ge(*c.same("y_f"))
                    if i:
                        low(i - 1)
                low(3)

                def out_slot(k, ahead):
                    if ahead:
                        split((k + 1) % 4)
                    dve.wait_ge(*c.take("tile_done"))
                    c.skip(f"bank{k % 2}")

                with Loop(dve, c, "out", 3):
                    for k in range(4):
                        out_slot(k, True)
                for k in range(4):
                    out_slot(k, k < 3)
                c.skip("misc_put")
                invert_rs()
                dve.wait_ge(*c.take("x_back", 16))
                with Loop(dve, c, "post", 4) as i:
                    y4 = mix[:, bass.ds(i * 4, 4), :]
                    link(tt(y4, y4, rs[:, :].unsqueeze(1).to_broadcast([P, 4, T]), ALU.mult))
                    for k in range(4):
                        xk = one(xv[:, bass.ds(i * 4 + k, 1), 0:SEQ])
                        stt(xk, one(mix[:, bass.ds(i * 4 + k, 1), 0:SEQ]), mod[:, bass.ds(i * 4 + (32 + k), 1), 0], xk,
                            ALU.mult, ALU.add).then_inc(*c.give("dve_step"))
                    ys, xs = samp(mix[:, bass.ds(i * 4, 4), SEQ:T]), samp(xv[:, bass.ds(i * 4, 4), SEQ:T])
                    link(tt(ys, ys, mod[:, bass.ds(i * 4 + 32, 4), 1:ROWS].unsqueeze(3).to_broadcast([P, 4, NB, TS]), ALU.mult))
                    tt(xs, xs, ys, ALU.add).then_inc(*c.give("x_tile", 4))

        @block.gpsimd
        def _(pool):
            c = Counts(pool, sems, per.setdefault("pool", {}))
            tt, cp = nc.gpsimd.tensor_tensor, nc.gpsimd.tensor_copy

            def link(ins):
                ins.then_inc(*c.give("pool_step"))
                pool.wait_ge(*c.same("pool_step"))

            def square(src, done=None):
                link(tt(sqp[:, :], src, src, ALU.mult))
                last = tt(acc[:, :], acc[:, :], sqp[:, :], ALU.add)
                if done:
                    last.then_inc(*c.give(done))
                    pool.wait_ge(*c.same(done))
                else:
                    link(last)

            def one(ap):
                return ap.rearrange("p a t -> p (a t)")

            for l in range(DEPTH):
                for b in range(NB):
                    pool.dma_start(win_s[l, b, 0:SEQ - TS].rearrange("t c g d -> t (c g d)"),
                                   cache_win[l, b, TS:SEQ].rearrange("t c g d -> t (c g d)")).then_inc(*c.give("stored2", 16))

            def squares_of_x():
                with Loop(pool, c, "xsq", 3) as i:
                    pool.wait_ge(*c.take("x_tile", 4))
                    for k in range(4):
                        square(one(xv[:, bass.ds(i * 4 + k, 1), :]))
                pool.wait_ge(*c.take("x_tile", 4))
                for k in range(12, 16):
                    square(xv[:, k, :], "ssq_ready" if k == 15 else None)

            link(nc.gpsimd.memset(sqp[:, :], 0.0))
            pool.wait_ge(*c.ahead("x_tile", KT))
            nc.gpsimd.memset(acc[:, :], 0.0).then_inc(*c.give("sq_free", 2))
            pool.wait_ge(*c.same("sq_free"))
            c.skip("misc_got", 2)
            squares_of_x()
            with Loop(pool, c, "layer", DEPTH) as l:
                c.skip("misc_got", 9)
                pool.wait_ge(*c.take("misc_got"))
                apart(pool)
                link(nc.gpsimd.memset(acc[:, :], 0.0))
                c.skip("misc_got", 5)
                pool.wait_ge(*c.take("kc_got"))
                with Loop(pool, c, "turn", 2) as g:
                    for br in range(2):
                        cp(vcur[:, br, :, :], vtok[:, br, 0:2, bass.ds(g * P, P)]).then_inc(*c.give("pool_step"))
                    cp(avc[:, 4 * NBLK:5 * NBLK], cact[:, 1, bass.ds(g * NBLK + NSEQ * NBLK, NBLK)]).then_inc(*c.give("v_turn"))

                    def pass_copies(pp):
                        for q in range(4):
                            cp(qs[:, q, 0:16].rearrange("p (r t) -> p r t", r=4),
                               mix[:, 8 + (q % 2) * 4:12 + (q % 2) * 4, bass.ds(g * 16 + (SEQ + 8 * pp + 4 * (q // 2)), TS)]).then_inc(
                                   *c.give("pool_step" if q < 3 else "qs_ready"))
                        cp(avc[:, 5 * NBLK:9 * NBLK], kcT[:, bass.ds(g * (8 * NBLK) + pp * 4 * NBLK, 4 * NBLK)]).then_inc(
                            *c.give("pool_step"))
                        cp(avc[:, 0:4 * NBLK], cact[:, 1, bass.ds(g * (8 * NBLK) + pp * 4 * NBLK, 4 * NBLK)]).then_inc(*c.give("av_ready"))

                    def query(h):
                        cp(qc[:, h % 2, :], one(mix[:, bass.ds(g * 4 + (8 + h), 1), 0:SEQ])).then_inc(*c.give("qc_ready"))

                    pass_copies(0)
                    query(0)
                    query(1)
                    pool.wait_ge(*c.take("op_put"))
                    query(2)
                    pool.wait_ge(*c.take("op_put"))
                    query(3)
                    pool.wait_ge(*c.take("os_put"))
                    pass_copies(1)
                    for m in range(2):
                        for ti in range(2):
                            pool.wait_ge(*c.take("ya_ready"))
                            square(one(mix[:, bass.ds(g * 4 + (2 * m + ti), 1), :]))
                    c.skip("op_put", 2)
                    pool.wait_ge(*c.take("os_put"))
                apart(pool)
                nc.gpsimd.memset(sqp[:, :], 0.0).then_inc(*c.give("a_done"))
                pool.wait_ge(*c.same("a_done"))
                pool.wait_ge(*c.take("misc_got"))
                apart(pool)
                link(nc.gpsimd.memset(acc[:, :], 0.0))
                with Loop(pool, c, "z", 2) as i:
                    for k in range(4):
                        pool.wait_ge(*c.take("yb_ready"))
                        square(one(mix[:, bass.ds(i * 4 + (8 + k), 1), :]))
                apart(pool)
                nc.gpsimd.memset(sqp[:, :], 0.0).then_inc(*c.give("b_done"))
                pool.wait_ge(*c.same("b_done"))
                pool.wait_ge(*c.take("misc_got"))
                apart(pool)
                link(nc.gpsimd.memset(acc[:, :], 0.0))
                with Loop(pool, c, "out", 4):
                    for k in range(4):
                        pool.wait_ge(*c.take("y_sq"))
                        tt(acc[:, :], acc[:, :], gz[:, k % 2, :], ALU.add).then_inc(*c.give("sq_free"))
                        pool.wait_ge(*c.same("sq_free"))
                apart(pool)
                nc.gpsimd.memset(sqp[:, :], 0.0).then_inc(*c.give("y_done"))
                pool.wait_ge(*c.same("y_done"))
                pool.wait_ge(*c.take("misc_got"))
                apart(pool)
                link(nc.gpsimd.memset(acc[:, :], 0.0))
                squares_of_x()
            pool.wait_ge(*c.same("stored2"))


_INS = ["x_prompt", "x_sample", "cache_kv", "cache_win", "state_conv", "page_table", "c_prompt", "c_sample", "w_ada",
        "b_ada", "g_pre", "w_in", "conv_w", "cmp_pe", "cmp_w1", "cmp_w2", "g_grp", "w_out", "g_post"]
_OUTS = [(1, SEQ, DM), (NB, TS, DM), (DEPTH, 1, SEQ, 4, NKV, HD), (DEPTH, NB, TS, 4, NKV, HD), (DEPTH, 1, SEQ, 2, NKV, HD),
         (DEPTH, NB, SEQ, 2, NKV, HD), (DEPTH, 1, 2, NC_CONV), (DEPTH, NB, 2, NC_CONV)]


def kernel(**inputs):
    import concourse.bacc as bacc
    from concourse.bass_utils import run_bass_kernel_spmd as run

    arrays = {f"in_{n}": np.ascontiguousarray(inputs[n]) for n in _INS}
    arrays["in_shape_constants"] = shape_constants()
    per = {}
    for final in (False, True):
        nc = bacc.Bacc("TRN2", target_bir_lowering=False, num_devices=1)
        ins = [nc.dram_tensor(n, a.shape, mybir.dt.from_np(a.dtype), kind="ExternalInput").ap() for n, a in arrays.items()]
        outs = [nc.dram_tensor(f"out_{i}", s, F32, kind="ExternalOutput").ap() for i, s in enumerate(_OUTS)]
        spill = nc.dram_tensor("x_scratch", (P, KT * T), F32, kind="Internal").ap()
        program(nc, per, ins[:-1], outs, ins[-1], spill)
        per_layer = {}
        for counts in per.values():
            for (name, loop), k in counts.items():
                if loop == "layer":
                    assert per_layer.setdefault(name, k) == k, (name, per_layer[name], k)
    r = run(nc, [arrays], core_ids=[0])
    return tuple(r.results[0][f"out_{i}"] for i in range(len(_OUTS)))
```

```python
from contextlib import ExitStack

import concourse.bass as bass
from concourse import mybir
import numpy as np

F32 = mybir.dt.float32
F32R = mybir.dt.float32r
ALU = mybir.AluOpType
ACT = mybir.ActivationFunctionType
AX_X = mybir.AxisListType.X

P = 128
DEPTH, DM, SEQ, NB, TS = 2, 2048, 256, 8, 4
KT = DM // P
HALF = KT // 2
NTS = NB * TS
T = SEQ + NTS
PAST, PAGE = 256, 128
NC_CONV, NH, NKV, HD = 1024, 8, 2, 128
GQA = NH // NKV
N_IN = 4 * NC_CONV + NH * HD + 6 * NKV * HD + 3 * NH + NH * HD
COL_Q, COL_KV = 4 * NC_CONV, 4 * NC_CONV + NH * HD
COL_G = COL_KV + 6 * NKV * HD
COL_Z = COL_G + 3 * NH
NG = 3 * NH
CMP_LEN, STRIDE, NBLK = 32, 16, 15
NSEQ = NB * NKV
NROW = T // STRIDE + NBLK
ROWS = 1 + NB
EPS, NEG = 1e-6, -1e30
SCALE = float(HD) ** -0.5
CH = 2 * P
N_SELECT, SEL_BLOCK, WINDOW = 8, 64, 512
assert max(-(-SEQ // SEL_BLOCK), N_SELECT) == N_SELECT == max(-(-(PAST + TS) // SEL_BLOCK), N_SELECT)
assert WINDOW > PAST + TS and (NBLK * STRIDE + CMP_LEN - 1) > PAST + TS - 1

C_ID, C_COS, C_SIN, C_TRI = 0, P, P + T, P + 2 * T
C_CMP = C_TRI + P
C_NEW = C_CMP + 2 * NBLK
C_GM = C_NEW + 4 * NTS
C_SUM = C_GM + NG
C_END = C_SUM + ROWS


def shape_constants():
    c = np.zeros((P, C_END), np.float32)
    c[:, C_ID:C_ID + P] = np.eye(P)
    half = HD // 2
    inv = np.power(np.float32(10000.0), -np.arange(half, dtype=np.float32) / np.float32(half))
    pos = np.concatenate([np.arange(SEQ), np.tile(PAST + np.arange(TS), NB)]).astype(np.float32)
    ang = (pos[None, :] * inv[:, None]).astype(np.float32)
    c[:, C_COS:C_COS + T] = np.concatenate([np.cos(ang), np.cos(ang)])
    c[:, C_SIN:C_SIN + T] = np.concatenate([np.sin(ang), -np.sin(ang)])
    r = np.arange(P)
    c[:, C_TRI:C_TRI + P] = np.where(r[None, :] <= r[:, None], 0.0, NEG)
    for i in range(2):
        ends = np.arange(NBLK) * STRIDE + CMP_LEN - 1
        c[:, C_CMP + i * NBLK:C_CMP + (i + 1) * NBLK] = np.where(ends[None, :] <= r[:, None] + i * P, 0.0, NEG)
    for p in range(4):
        for q in range(NTS):
            b, t = q // TS, q % TS
            ok = (b == 2 * p + r // 64) & (t <= r % TS)
            c[:, C_NEW + p * NTS + q] = np.where(ok, 0.0, NEG)
    for col in range(NG):
        head = col // 3
        c[:, C_GM + col] = (head == ((r // 32) % 2) * GQA + (r % 32) // TS) & (r % 32 < GQA * TS)
    for i in range(2 * ROWS):
        c[i, C_SUM + i % ROWS] = 1.0
    return c


class Counts:

    def __init__(self, eng, sems, per):
        self.eng, self.sems, self.per = eng, sems, per
        self.n = {}
        self.loops = []

    def value(self, name):
        v = self.n.get(name, 0)
        for loop, i in self.loops:
            k = self.per.get((name, loop), 0)
            if k:
                v = i * k + v
        return v

    def take(self, name, k=1):
        self.n[name] = self.n.get(name, 0) + k
        return self.sems[name], self.value(name)

    def give(self, name, k=1):
        self.n[name] = self.n.get(name, 0) + k
        return self.sems[name], k

    def same(self, name):
        return self.sems[name], self.value(name)

    def ahead(self, name, k=1):
        return self.sems[name], self.value(name) + k

    def skip(self, name, k=1):
        self.n[name] = self.n.get(name, 0) + k

    def enter(self, loop, i):
        self.loops.append((loop, i))
        return dict(self.n)

    def leave(self, loop, before, trips):
        self.loops.pop()
        for name in self.n:
            d = self.n[name] - before.get(name, 0)
            known = self.per.setdefault((name, loop), d)
            assert known == d, (name, loop, known, d)
            self.n[name] = before.get(name, 0) + trips * d


PROMPT = {s: (s // 3, s % 3) for s in range(12)}
SAMPLE = {0: (0, 0), 2: (0, 1), 4: (0, 2), 7: (1, 0), 9: (1, 1), 11: (1, 2)}
KTURN = {s: pk for s, pk in SAMPLE.items() if pk[1] < 2}
VTURN = {s: pk for s, pk in SAMPLE.items() if pk[1] == 2}
GATE = (1, 2, 0)

SEMS = """crow0 crow1 crow_used w1_in0 w1_in1 w1_in2 w1_in3 w1_used apart a_done act_step av_ready b_done bank0 bank1 c_done c_in c_tanh cache0 cache1 cache2 cache3 cache_used cmp_a
cmp_h cmp_row cmp_put cmp_tanh const_in dve_step fin_put0 fin_put1 gate_ready graw h_hi h_ready h_p h_s hi_ready kc_got kc_put
kv_done lo_ready mem_set misc_got misc_put mod_row op_got op_put os_got os_put pool_step pt_got pt_put pts_got
pts_put qc_ready qs_ready raw00 raw01 raw10 raw11 sp_e sp_nm sp_p sp_put sq_free ss_e ss_nm ss_p ss_put ssq_ready rs_ready stored
stored2 tile_done tp_got tp_put u_put v_ready v_turn vec_in x_back x_in x_last x_put0 x_put1 x_spill x_tile xn y_done y_f
y_hi y_hl y_sq ya_ready yb_ready z_t""".split()


def program(nc, per, ins, outs, consts, spill):
    (x_prompt, x_sample, cache_kv, cache_win, state_conv, page_table, c_prompt, c_sample, w_ada, b_ada, g_pre,
     w_in, conv_w, cmp_pe, cmp_w1, cmp_w2, g_grp, w_out, g_post) = ins
    y_p, y_s, kv_p, kv_s, win_p, win_s, conv_p, conv_s = outs

    with ExitStack() as ctx:
        def sb(name, shape, dt=F32):
            return ctx.enter_context(nc.sbuf_tensor(name, shape, dt))

        raw = sb("raw", [P, 2, KT * CH])
        w_hi = sb("w_hi", [P, 2, KT, P], F32R)
        w_lo = sb("w_lo", [P, 2, KT, P], F32R)
        xT = sb("xT", [P, KT * T])
        h_hi = sb("h_hi", [P, KT, T], F32R)
        h_lo = sb("h_lo", [P, KT, T], F32R)
        mix = sb("mix", [P, KT, T])
        heads = sb("heads", [P, 8 * T + 2 * T + 448 + 6 * CH])
        lent = sb("lent", [P, 2 * CMP_LEN // 4 * P + 2048])
        stage = sb("stage", [P, 3, CH])
        cbuf = sb("cbuf", [P, 2, T])
        ubuf = sb("ubuf", [P, 2, 2 + SEQ + NB * (TS + 2)])
        gz = sb("gz", [P, 2, T])
        qs = sb("qs", [P, 4, 32])
        cst = sb("cst", [P, C_END])
        ones = sb("ones", [P, P])
        vec = sb("vec", [P, 120])
        w2 = sb("w2", [P, 2, P])
        mod = sb("mod", [P, 48, ROWS])
        cHL = sb("cHL", [P, KT, 2 * ROWS], F32R)
        kcT = sb("kcT", [P, (NSEQ + 2) * NBLK])
        cact = sb("cact", [P, 2, (NSEQ + 2) * NBLK])
        vcs = sb("vcs", [NBLK, 4, P])
        vcp = sb("vcp", [NBLK, P])
        avc = sb("avc", [P, 9 * NBLK])
        stT = sb("stT", [P, 8, 2 * NB])
        uo = sb("uo", [P, 8, 2 + 2 * NB])
        acc = sb("acc", [P, T])
        sqp = sb("sqp", [P, T])
        accb = sb("accb", [P, T])
        rs = sb("rs", [P, T])
        ra = sb("ra", [P, T])
        gtok = sb("gtok", [P, 2, NG])
        gsm = sb("gsm", [P, 4, 3])
        mrow = sb("mrow", [2 * ROWS, 2, P])
        small = sb("small", [P, 16])
        pages = sb("pages", [1, NB * 2], mybir.dt.int32)

        kvf = heads[:, 0:8 * T]
        kvT = kvf.rearrange("p (k t) -> p k t", t=T)
        vq = heads[:, 8 * T:10 * T + 448]
        vtok = heads[:, 10 * T + 448:].rearrange("p (b i d) -> p b i d", b=2, i=3)
        X = lent[:, 0:8 * PAGE].rearrange("p (a b) -> p a b", a=4)
        prob = lent[:, 1024:1792].rearrange("p (a b) -> p a b", a=2)
        sprobT, probT, sprob = lent[:, 1792:2176], lent[:, 2176:2560], lent[:, 2560:2560 + T]
        mixf = mix[:, :, :].rearrange("p k t -> p (k t)")
        ring = xT[:, 0:4096].rearrange("p (s g d) -> p s g d", s=4, g=2)
        graw = xT[:, 4096:4096 + KT * NG].rearrange("p (k n) -> p k n", k=KT)
        xv = xT[:, :].rearrange("p (k t) -> p k t", k=KT)
        rawv = [raw[:, s, :].rearrange("p (k n) -> p k n", k=KT) for s in range(2)]
        past = [mixf[:, 0:17 * 2 * PAGE], heads[:, 0:17 * 2 * PAGE]]
        past = [a.rearrange("p (q t) -> p q t", t=2 * PAGE) for a in past]
        w1s = lent[:, 0:4096].rearrange("p (q j n) -> p q j n", n=P, j=CMP_LEN // 4)
        crow = lent[:, 2048:4096].rearrange("p (s g d) -> p s g d", s=2, g=2)
        vtmp = vq[:, 0:2 * T].rearrange("p (s t) -> p s t", s=2)
        vcur = vq[:, 0:512].rearrange("p (b i d) -> p b i d", b=2, i=2)
        qc = vq[:, 512:1024].rearrange("p (s t) -> p s t", s=2)
        kwork = X
        yp, ys = raw[:, 0, :].rearrange("p (i n) -> p i n", i=2), raw[0:NTS, 1, 0:DM]
        ident = cst[:, C_ID:C_ID + P]
        tri = cst[:, C_TRI:C_TRI + P]
        eps = small[:, 15:16]
        xsrow = X[0:2 * NB, 0:4, :].rearrange("p a b -> p (a b)")

        uorow = X[0:2 + 2 * NB, 0:4, :].rearrange("p a b -> p (a b)")

        ps = [ctx.enter_context(nc.psum_tensor(f"ps{i}", [P, 512], F32)) for i in range(8)]
        proj = [ps[0], ps[1]]
        pmisc, ptr, pS, pSs, pPT, pO = ps[2], ps[3], ps[4], ps[5], ps[6], ps[7]
        pOs = pmisc
        pB = [pS, pSs]

        sems = {n: ctx.enter_context(nc.semaphore(n)) for n in SEMS}
        block = ctx.enter_context(nc.Block())

        def apart(eng):
            eng.sem_inc(sems["apart"], 1)

        class Loop:

            def __init__(self, eng, c, name, trips):
                self.eng, self.c, self.name, self.trips = eng, c, name, trips

            def __enter__(self):
                apart(self.eng)
                self.f = self.eng.Fori(0, self.trips)
                i = self.f.__enter__()
                self.before = self.c.enter(self.name, i)
                return i

            def __exit__(self, *a):
                if a[0]:
                    return False
                self.c.leave(self.name, self.before, self.trips)
                return self.f.__exit__(*a)

        @block.sync
        def _(sp):
            c = Counts(sp, sems, per.setdefault("sp", {}))
            sp.dma_start(cst[:, :], consts).then_inc(*c.give("const_in", 16))
            sp.dma_start(mixf[0:1, DM:2 * DM], c_prompt).then_inc(*c.give("c_in", 16))
            sp.dma_start(mixf[1:ROWS, DM:2 * DM], c_sample).then_inc(*c.give("c_in", 16))
            sp.dma_start(pages[:, :], page_table.rearrange("b (o g) -> o (b g)", o=1)).then_inc(*c.give("const_in", 16))
            for i in range(2):
                sp.dma_start(heads[:, i * DM:(i + 1) * DM], x_prompt[0, i * P:(i + 1) * P, :]).then_inc(*c.give("x_in", 16))
            sp.dma_start(lent[0:NTS, 2048:2048 + DM], x_sample.rearrange("b t d -> (b t) d")).then_inc(*c.give("x_in", 16))
            sp.wait_ge(*c.same("const_in"))

            def chunk(slot, src):
                for h in range(2):
                    sp.wait_ge(*c.take("lo_ready", 1 if h else 3))
                    apart(sp)
                    rows = slice(h * HALF, (h + 1) * HALF)
                    sp.dma_start(rawv[slot][:, rows, :], src[:, rows, :]).then_inc(*c.give(f"raw{slot}{h}", 16))

            def wcols(w, l, col):
                return w[bass.ds(l, 1), :, bass.ds(col, CH)].rearrange("l (k p) n -> p (l k) n", p=P)

            def load_cache(l, b, slot, kind, sem):
                for pg in range(2):
                    if kind == "win":
                        src = cache_win[bass.ds(l, 1), bass.ds(b, 1), pg * PAGE:(pg + 1) * PAGE].rearrange(
                            "l b t c g d -> (l b t) (c g d)")
                    else:
                        apart(sp)
                        page = sp.value_load(pages[0:1, bass.ds(b * 2 + pg, 1)], min_val=0, max_val=cache_kv.shape[1] - 1)
                        lo = 0 if kind == "cmp" else 2
                        src = cache_kv[bass.ds(l, 1), bass.ds(page, 1), :, lo:lo + 2].rearrange(
                            "l n t c g d -> (l n t) (c g d)")
                    sp.dma_start((crow if kind == "cmp" else ring)[:, slot, pg, :], src).then_inc(*c.give(sem, 16))

            def load_w1(l, q, slot):
                sp.dma_start(w1s[:, slot, :, :], cmp_w1[bass.ds(l, 1), q // 4, q % 4 * (CMP_LEN * P // 4):(q % 4 + 1) * (CMP_LEN * P // 4)].rearrange(
                    "l (j d) n -> d (l j) n", d=P)).then_inc(*c.give(f"w1_in{slot}", 16))

            def load_pass(l, n, kind):
                sp.wait_ge(*c.take("cache_used"))
                for b in range(2):
                    load_cache(l, 2 * n + b, 2 * kind + b, ("slc", "win")[kind], f"cache{2 * kind + b}")

            with Loop(sp, c, "layer", DEPTH) as l:
                for lo, src in ((0, b_ada), (48, g_pre), (64, g_grp), (80, g_post)):
                    n = src.shape[1] // P
                    sp.dma_start(stage[lo:lo + n, 0, 0:P], src[bass.ds(l, 1), :].rearrange(
                        "l (k p) -> (l k) p", p=P)).then_inc(*c.give("vec_in", 16))
                sp.dma_start(stage[96:120, 0, 0:P], conv_w[bass.ds(l, 1)].rearrange(
                    "l i (k p) -> (l i k) p", p=P)).then_inc(*c.give("vec_in", 16))
                sp.dma_start(stage[0:64, 1, 0:P], cmp_pe[bass.ds(l, 1)].rearrange("l i j d -> (l i j) d")).then_inc(
                    *c.give("vec_in", 16))
                sp.dma_start(xsrow, state_conv[bass.ds(l, 1)].rearrange("l b i n -> (l b i) n")).then_inc(*c.give("vec_in", 16))
                sp.dma_start(w2[:, :, :], cmp_w2[bass.ds(l, 1)].rearrange("l i k n -> k (l i) n")).then_inc(*c.give("vec_in", 16))
                with Loop(sp, c, "shift", 4) as i:
                    for s in range(2):
                        chunk(s, wcols(w_ada, l, i * 512 + s * CH))
                        sp.wait_ge(*c.take("crow_used"))
                        load_cache(l, i * 2 + s, s, "cmp", f"crow{s}")
                for t in range(16):
                    if t % 2 == 0:
                        chunk(t // 2 % 2, wcols(w_ada, l, DM + t * P))
                        if t > 2:
                            sp.wait_ge(*c.take("w1_used"))
                        load_w1(l, t // 2, t // 2 % 2)
                sp.wait_ge(*c.take("ssq_ready"))
                with Loop(sp, c, "ada2", 4) as i:
                    for s in range(2):
                        chunk(s, wcols(w_ada, l, i * 512 + s * CH + 2 * DM))
                for i in range(5):
                    for s in range(2):
                        chunk(s, wcols(w_in, l, COL_Q + (2 * i + s) * CH))
                        if i == 0 and s == 1:
                            sp.dma_start(spill, xT[:, :]).then_inc(*c.give("x_spill", 16))
                        if i in (1, 2) and s == 1:
                            if i == 1:
                                sp.wait_ge(*c.take("w1_used", 2))
                            for q in (2 * i - 2, 2 * i - 1):
                                load_w1(l, q, q)
                        if i == 3 and s == 0:
                            sp.wait_ge(*c.same("x_spill"))
                            sp.wait_ge(*c.take("h_ready", 4))
                            sp.dma_start(graw, w_in[bass.ds(l, 1), :, COL_G:COL_G + NG].rearrange(
                                "l (k p) n -> p (l k) n", p=P)).then_inc(*c.give("graw", 16))
                        if i == 4:
                            sp.wait_ge(*c.take("w1_used"))
                            load_w1(l, 4 + s, s)
                for n in range(4):
                    g, m = n // 2, n % 2
                    for kind, off in enumerate((1, 2, 3, 0)):
                        chunk(kind % 2, wcols(w_in, l, off * NC_CONV + g * 512 + m * CH))
                        if n and kind < 2:
                            load_pass(l, n, kind)
                        if n == 0 and kind < 2:
                            sp.wait_ge(*c.take("w1_used"))
                            load_w1(l, 6 + kind, 2 + kind)
                            load_pass(l, 0, kind)
                        if n == 0 and kind == 1:
                            c.skip("lo_ready", 2)
                for i in range(2):
                    for s in range(2):
                        chunk(s, wcols(w_in, l, COL_Z + (2 * i + s) * CH))
                sp.wait_ge(*c.ahead("cache_used", 2))
                sp.dma_start(xT[:, :], spill).then_inc(*c.give("x_back", 16))
                with Loop(sp, c, "out", 4) as i:
                    for s in range(2):
                        chunk(s, wcols(w_out, l, i * 512 + s * CH))
                c.skip("w1_used", 4)

        @block.tensor
        def _(pe):
            c = Counts(pe, sems, per.setdefault("pe", {}))
            mm, tr = nc.tensor.matmul, nc.tensor.transpose
            pe.wait_ge(*c.take("const_in", 32))
            pe.wait_ge(*c.take("mem_set"))
            pe.wait_ge(*c.take("misc_got"))
            pe.wait_ge(*c.take("c_done"))
            for k in range(KT):
                last = tr(pmisc[:, k * ROWS:(k + 1) * ROWS], mixf[0:ROWS, k * P:(k + 1) * P], ident[0:ROWS, 0:ROWS])
            last.then_inc(*c.give("misc_put"))
            pe.wait_ge(*c.take("x_in", 48))
            for k in range(KT):
                b = k % 2
                pe.wait_ge(*c.take(f"bank{b}"))
                for i in range(2):
                    tr(proj[b][:, i * P:(i + 1) * P], heads[:, i * DM + k * P:i * DM + (k + 1) * P], ident)
                tr(proj[b][:, SEQ:T], lent[0:NTS, 2048 + k * P:2048 + (k + 1) * P], ident[0:NTS, 0:NTS]).then_inc(*c.give(f"x_put{b}"))
            c.skip("lo_ready", 8)
            pe.sem_inc(*c.give("cache_used", 2))
            pe.wait_ge(*c.same("x_put0"))
            pe.wait_ge(*c.same("x_put1"))
            pe.sem_inc(*c.give("crow_used", 2))

            def tile(s, width=P):
                pe.wait_ge(*c.take(f"bank{s}"))
                out = proj[s][0:width, 0:T]
                for k in range(KT):
                    if k % HALF == 0:
                        pe.wait_ge(*c.take("lo_ready"))
                    mm(out, w_hi[:, s, k, 0:width], h_hi[:, k, :], start=(k == 0), stop=False)
                    mm(out, w_hi[:, s, k, 0:width], h_lo[:, k, :], start=False, stop=False)
                    last = mm(out, w_lo[:, s, k, 0:width], h_hi[:, k, :], start=False, stop=(k == KT - 1))
                last.then_inc(*c.give("tile_done"))

            def out_tile(s, first=False):
                pe.wait_ge(*c.take(f"bank{s}"))
                for k in range(KT):
                    if k % HALF == 0:
                        pe.wait_ge(*c.take("lo_ready"))
                    if first and k % 4 == 0:
                        pe.wait_ge(*c.take("y_hl"))
                    out = (proj[s], pB[s])[k // HALF][:, 0:T]
                    mm(out, w_hi[:, s, k, :], h_hi[:, k, :], start=(k % HALF == 0), stop=False)
                    mm(out, w_hi[:, s, k, :], h_lo[:, k, :], start=False, stop=False)
                    last = mm(out, w_lo[:, s, k, :], h_hi[:, k, :], start=False, stop=(k % HALF == HALF - 1))
                last.then_inc(*c.give("tile_done"))

            def mod_tile(s):
                for k in range(KT):
                    if k % HALF == 0:
                        pe.wait_ge(*c.take("lo_ready"))
                    mm(proj[s][0:2 * ROWS, 0:P], cHL[:, k, :], w_hi[:, s, k, :], start=(k == 0), stop=False)
                    last = mm(proj[s][0:2 * ROWS, 0:P], cHL[:, k, :], w_lo[:, s, k, :], start=False, stop=(k == KT - 1))
                last.then_inc(*c.give("tile_done"))

            def mod_turn(j):
                pe.wait_ge(*c.take("mod_row"))
                last = mm(pmisc[:, j * ROWS:(j + 1) * ROWS], mrow[:, j % 2, :], cst[0:2 * ROWS, C_SUM:C_END],
                          start=True, stop=True)
                if j == 3:
                    last.then_inc(*c.give("misc_put"))

            def mod_tiles(before_turn=None):
                for j in range(4):
                    mod_tile(j % 2)
                    if before_turn:
                        before_turn(j)
                    if j == 1:
                        pe.wait_ge(*c.take("misc_got"))
                    if j:
                        mod_turn(j - 1)
                mod_turn(3)

            def past_turn(j):
                slot, is_v = j // 2, j % 2
                if j:
                    pe.wait_ge(*c.take("tp_got"))
                if not is_v:
                    pe.wait_ge(*c.take(f"crow{slot}", 32))
                for gg in range(NKV):
                    for pg in range(2):
                        last = tr(ptr[:, (gg * 2 + pg) * P:(gg * 2 + pg + 1) * P],
                                  crow[:, slot, pg, is_v * CH + gg * P:is_v * CH + (gg + 1) * P], ident)
                last.then_inc(*c.give("tp_put"))
                if is_v:
                    pe.wait_ge(*c.same("tp_put"))
                    pe.sem_inc(*c.give("crow_used"))

            def hidden_part(t):
                i, j0 = t // 8, t % 8 * 4
                if t % 2 == 0:
                    pe.wait_ge(*c.take(f"w1_in{t // 2 % 2}", 16))
                if t == 8:
                    pe.wait_ge(*c.take("cmp_h"))
                for j in range(j0, j0 + 4):
                    last = mm(pSs[:, 0:17 * NBLK], w1s[:, t // 2 % 2, j % 8, :], past[i][:, :, j:j + 225:STRIDE],
                              start=(j == 0), stop=(j == CMP_LEN - 1))
                if t % 8 == 7:
                    last.then_inc(*c.give("cmp_put"))
                    pe.wait_ge(*c.same("cmp_put"))
                    pe.sem_inc(*c.give("w1_used"))
                elif t % 2:
                    last.then_inc(*c.give("w1_used"))

            def sum_squares(ready, src=acc):
                pe.wait_ge(*c.take(ready))
                pe.wait_ge(*c.take("misc_got"))
                mm(pmisc[:, 0:T], ones[:, :], src[:, :], start=True, stop=True).then_inc(*c.give("misc_put"))

            def kv_turn(j):
                is_v = (j % 4) // 2
                pe.wait_ge(*c.take("v_ready" if is_v else "kv_done"))
                if j:
                    pe.wait_ge(*c.take("tp_got"))
                src = vtmp[:, j % 2, :] if (j >= 4 and is_v) else kvT[:, (0, 4, 6)[j // 4] + (j % 4), :]
                for i in range(2):
                    tr(ptr[:, i * P:(i + 1) * P], src[:, i * P:(i + 1) * P], ident)
                tr(ptr[0:NTS, SEQ:SEQ + P], src[:, SEQ:T], ident).then_inc(*c.give("tp_put"))

            def prompt_hidden(q):
                i, w = q // 4, q % 4
                pe.wait_ge(*c.take(f"w1_in{w}", 16))
                for j in range(w * 8, w * 8 + 8):
                    at = 2 * i * T + j
                    last = mm((pSs, pPT)[i][0:NROW, 0:P], kvf[:, at:at + (NROW - 1) * STRIDE + 1:STRIDE],
                              w1s[:, w, j % 8, :], start=(j == 0), stop=(j == CMP_LEN - 1))
                if w < 3:
                    last.then_inc(*c.give("w1_used"))
                else:
                    last.then_inc(*c.give("cmp_put"))
                    pe.wait_ge(*c.same("cmp_put"))
                    pe.sem_inc(*c.give("w1_used"))

            def prompt_turn(i):
                pe.wait_ge(*c.take("cmp_row"))
                apart(pe)
                tr((pSs, pPT)[i][:, 256:256 + NROW], gz[0:NROW, 1, i * P:(i + 1) * P], ident[0:NROW, 0:NROW]).then_inc(
                    *c.give("cmp_put"))

            def pe_before(s, g):
                if s == 1:
                    pe.wait_ge(*c.same("kc_got"))
                    pe.wait_ge(*c.take("v_turn"))
                    pe.wait_ge(*c.take("tp_got"))
                    mm(ptr[0:NBLK, 0:P], avc[:, 4 * NBLK:5 * NBLK], w2[:, 1, :], start=True, stop=True).then_inc(
                        *c.give("tp_put"))
                if s in KTURN:
                    k_turn(s, 0)

            def k_turn(s, b):
                slot = 2 * (KTURN[s][1]) + b
                pe.wait_ge(*c.take(f"cache{slot}", 32))
                for gg in range(NKV):
                    for pg in range(2):
                        last = tr(ptr[:, (gg * 2 + pg) * P:(gg * 2 + pg + 1) * P], ring[:, slot, pg, gg * P:(gg + 1) * P], ident)
                last.then_inc(*c.give("tp_put"))

            def pe_tasks(s, g):
                if s - 2 in PROMPT:
                    head, kind = PROMPT[s - 2]
                    pe.wait_ge(*c.take("pt_got"))
                    if kind < 2:
                        if kind == 0:
                            pe.wait_ge(*c.take("op_got"))
                        mm(pO[:, 0:SEQ], vcur[:, kind, 0, :], probT[:, 0:SEQ], start=(kind == 0), stop=False, skip_group_check=True)
                        mm(pO[:, P:SEQ], vcur[:, kind, 1, :], probT[:, SEQ:3 * P], start=False, stop=False, skip_group_check=True)
                    else:
                        mm(pO[:, 0:SEQ], vcp[:, :], probT[0:NBLK, 0:SEQ], start=False, stop=True,
                           skip_group_check=True).then_inc(*c.give("op_put"))
                if s in PROMPT:
                    head, kind = PROMPT[s]
                    if kind == 0:
                        pe.wait_ge(*c.take("qc_ready"))
                    pe.wait_ge(*c.take("sp_e"))
                    q = qc[:, head % 2, :]
                    if kind < 2:
                        mm(pS[:, 0:P], q[:, 0:P], kvT[:, bass.ds(g + (4 + 2 * kind), 1), 0:P].rearrange("p a t -> p (a t)"), start=True, stop=True)
                        mm(pS[:, P:3 * P], q[:, P:SEQ], kvT[:, bass.ds(g + (4 + 2 * kind), 1), 0:SEQ].rearrange("p a t -> p (a t)"), start=True,
                           stop=True).then_inc(*c.give("sp_put"))
                    else:
                        kc = kcT[:, bass.ds(g * NBLK + NSEQ * NBLK, NBLK)]
                        mm(pS[:, 0:NBLK], q[:, 0:P], kc, start=True, stop=True)
                        mm(pS[:, NBLK:2 * NBLK], q[:, P:SEQ], kc, start=True, stop=True).then_inc(*c.give("sp_put"))
                if s - 1 in PROMPT:
                    head, kind = PROMPT[s - 1]
                    pr = prob[:, (s - 1) % 2, :]
                    pe.wait_ge(*c.take("sp_p"))
                    if kind < 2:
                        for i in range(3):
                            last = tr(pPT[:, i * P:(i + 1) * P], pr[:, i * P:(i + 1) * P], ident)
                    else:
                        for i in range(2):
                            last = tr(pPT[0:NBLK, i * P:(i + 1) * P], pr[:, i * NBLK:(i + 1) * NBLK], ident)
                    last.then_inc(*c.give("pt_put"))
                if s in KTURN:
                    pe.wait_ge(*c.take("tp_got"))
                    k_turn(s, 1)
                if s in VTURN:
                    pe.wait_ge(*c.take("av_ready"))
                    for q in range(4):
                        last = mm(ptr[0:NBLK, q * P:(q + 1) * P], avc[:, q * NBLK:(q + 1) * NBLK], w2[:, 1, :], start=True, stop=True)
                    last.then_inc(*c.give("tp_put"))
                if s - 3 in SAMPLE:
                    pp, kind = SAMPLE[s - 3]
                    pe.wait_ge(*c.take("pts_got"))
                    if kind == 0:
                        pe.wait_ge(*c.take("os_got"))
                    for q in range(4):
                        b, gg = q // 2, q % 2
                        o = pOs[:, q * 16:(q + 1) * 16]
                        if kind < 2:
                            for pg in range(2):
                                mm(o, ring[:, 2 * kind + b, pg, CH + gg * P:CH + (gg + 1) * P],
                                   sprobT[:, pg * P + q * 32:pg * P + q * 32 + 16], start=(kind == 0 and q == 0 and pg == 0),
                                   stop=False, skip_group_check=True)
                            last = mm(o, vtok[0:NTS, kind, 2, gg * P:(gg + 1) * P], sprobT[0:NTS, SEQ + q * 32:SEQ + q * 32 + 16],
                                      start=False, stop=False, skip_group_check=True)
                        else:
                            last = mm(o, vcs[:, q, :], sprobT[0:NBLK, q * 32:q * 32 + 16], start=False, stop=(q == 3),
                                      skip_group_check=True)
                    last.then_inc(*c.give("cache_used" if kind < 2 else "os_put"))
                if s - 1 in SAMPLE:
                    pp, kind = SAMPLE[s - 1]
                    pe.wait_ge(*c.take("tp_got"))
                    if kind == 0:
                        pe.wait_ge(*c.take("qs_ready"))
                    for q in range(4):
                        o = pSs[q * 32:(q + 1) * 32, :]
                        if kind < 2:
                            mm(o[:, 0:SEQ], qs[:, q, :], kwork[:, q, :], start=True, stop=True)
                            last = mm(o[:, SEQ:T], qs[:, q, :], kvT[:, 4 + 2 * kind + q % 2, SEQ:T], start=True, stop=True)
                        else:
                            last = mm(o[:, 0:NBLK], qs[:, q, :], avc[:, (5 + q) * NBLK:(6 + q) * NBLK], start=True, stop=True)
                    last.then_inc(*c.give("ss_put"))
                if s - 2 in SAMPLE:
                    pp, kind = SAMPLE[s - 2]
                    pe.wait_ge(*c.take("ss_p"))
                    if kind < 2:
                        for i in range(2):
                            tr(pSs[:, i * P:(i + 1) * P], sprob[:, i * P:(i + 1) * P], ident)
                        last = tr(pSs[0:NTS, SEQ:SEQ + P], sprob[:, SEQ:T], ident)
                    else:
                        last = tr(pSs[0:NBLK, 0:P], sprob[:, 0:NBLK], ident)
                    last.then_inc(*c.give("pts_put"))

            with Loop(pe, c, "layer", DEPTH) as l:
                pe.wait_ge(*c.take("vec_in", 128))
                pe.wait_ge(*c.take("misc_got"))
                tr(pmisc[:, 0:120], stage[0:120, 0, 0:P], ident[0:120, 0:120])
                tr(pmisc[:, 128:192], stage[0:64, 1, 0:P], ident[0:64, 0:64])
                for k in range(8):
                    last = tr(pmisc[:, 192 + k * 16:208 + k * 16], xsrow[:, k * P:(k + 1) * P], ident[0:16, 0:16])
                last.then_inc(*c.give("misc_put"))
                for s in range(2):
                    pe.wait_ge(*c.ahead(f"bank{s}"))
                with Loop(pe, c, "shift", 4):
                    mod_tiles(past_turn)
                    pe.wait_ge(*c.take("tp_got"))
                for q in range(4):
                    mod_tiles(lambda j: hidden_part(4 * q + j))
                sum_squares("ssq_ready")
                with Loop(pe, c, "ada2", 4):
                    mod_tiles()
                pe.wait_ge(*c.take("h_ready", 4))
                with Loop(pe, c, "q", 2):
                    for s in range(4):
                        tile(s % 2)
                for j in range(12):
                    tile(j % 2)
                    if j:
                        kv_turn(j - 1)
                    if j == 4:
                        pe.wait_ge(*c.take("cmp_h"))
                    if j >= 4:
                        prompt_hidden(j - 4)
                    if j == 9:
                        prompt_turn(0)
                tile(0, NG)
                kv_turn(11)
                prompt_turn(1)
                pe.wait_ge(*c.take("tp_got"))
                pe.wait_ge(*c.take("gate_ready"))
                pe.wait_ge(*c.take("misc_got"))
                apart(pe)
                for i in range(2):
                    tr(pmisc[:, i * NG:(i + 1) * NG], cbuf[0:NG, 0, i * P:(i + 1) * P], ident[0:NG, 0:NG])
                gx = ubuf[0:NG, :, :].rearrange("p a b -> p (a b)")
                for p in range(4):
                    last = tr(pmisc[:, 48 + p * NG:48 + (p + 1) * NG], gx[:, p * P:(p + 1) * P], ident[0:NG, 0:NG])
                last.then_inc(*c.give("misc_put"))
                pe.wait_ge(*c.take("cmp_h", 2))
                pe.wait_ge(*c.take("cmp_a"))
                mm(pSs[:, 0:(NSEQ + 2) * NBLK], w2[:, 0, :], cact[:, 0, :], start=True, stop=True).then_inc(*c.give("kc_put"))
                c.skip("kc_got")

                with Loop(pe, c, "turn", 2) as g:
                    for s in range(16):
                        pe_before(s, g)
                        tile(s % 2)
                        pe_tasks(s, g)
                with Loop(pe, c, "z", 2):
                    for s in range(4):
                        tile(s % 2)
                out_tile(0, True)
                sum_squares("a_done")
                sum_squares("b_done", accb)
                pe.wait_ge(*c.take("u_put"))
                for half in range(2):
                    for k in range(4):
                        last = tr(ptr[0:2 + 2 * NB, k * P:(k + 1) * P], uo[:, half * 4 + k, :], ident)
                    last.then_inc(*c.give("tp_put"))
                    pe.wait_ge(*c.take("tp_got"))
                for s in range(1, 4):
                    out_tile(s % 2)
                with Loop(pe, c, "out", 3):
                    for s in range(4):
                        out_tile(s % 2)
                sum_squares("y_done")
            for k in range(KT):
                b = k % 2
                if k == 12:
                    pe.wait_ge(*c.take("x_last", 1 + DEPTH))
                elif k % 4 == 0:
                    pe.wait_ge(*c.take("x_tile", 4 if k else 12 * DEPTH + 4))
                pe.wait_ge(*c.take(f"bank{b}"))
                for i in range(2):
                    tr(proj[b][:, i * P:(i + 1) * P], xv[:, k, i * P:(i + 1) * P], ident)
                tr(proj[b][0:NTS, SEQ:SEQ + P], xv[:, k, SEQ:T], ident).then_inc(*c.give(f"fin_put{b}"))

        @block.scalar
        def _(act):
            c = Counts(act, sems, per.setdefault("act", {}))
            fn = nc.scalar.activation

            def copy(out, in_, scale=1.0):
                return fn(out, in_, ACT.Copy, scale=scale)

            def one(ap):
                return ap.rearrange("p a t -> p (a t)")

            def split(k):
                for h in (slice(0, HALF), slice(HALF, KT)):
                    if k % 2 == 0:
                        act.wait_ge(*c.take(f"raw{k // 2 % 2}{h.start // HALF}", 16))
                    copy(w_hi[:, k % 2, h, :], rawv[k // 2 % 2][:, h, (k % 2) * P:(k % 2 + 1) * P]).then_inc(*c.give("hi_ready"))

            def rstd(n=DM, dst=rs):
                act.wait_ge(*c.take("misc_put"))
                fn(dst[:, :], pmisc[:, 0:T], ACT.Sqrt, scale=1.0 / n, bias=eps).then_inc(*c.give("misc_got"))

            act.wait_ge(*c.take("c_in", 32))
            fn(mixf[0:ROWS, 0:DM], mixf[0:ROWS, DM:2 * DM], ACT.Tanh, scale=0.5).then_inc(*c.give("c_tanh"))
            act.wait_ge(*c.take("mem_set"))
            act.sem_inc(*c.give("sp_e"))
            c.skip("misc_put")
            c.skip("misc_got", 2)
            c.skip("bank0", 1 + KT // 2)
            c.skip("bank1")
            for k in range(1, KT, 2):
                act.wait_ge(*c.take("x_put1"))
                copy(xv[:, k, :], proj[1][:, 0:T]).then_inc(*c.give("bank1"))

            def mod_slots():
                c.skip("misc_put")
                for k in range(4):
                    act.wait_ge(*c.take("tile_done"))
                    copy(mrow[:, k % 2, :], proj[k % 2][0:2 * ROWS, 0:P]).then_inc(*c.give("mod_row"))
                    split((k + 2) % 4)
                    yield k
                c.skip("misc_got")

            def past_turned(i, j):
                act.wait_ge(*c.take("tp_put"))
                copy(past[j % 2][:, bass.ds(i * 4 + j // 2 * 2, 2), :], ptr[:, :].rearrange("p (g t) -> p g t", g=2)).then_inc(
                    *c.give("tp_got"))

            def hidden_tanh():
                act.wait_ge(*c.take("cmp_h"))
                fn(gz[:, 0, 0:2 * NBLK], cbuf[:, 1, 0:2 * NBLK], ACT.Tanh, scale=0.5).then_inc(*c.give("cmp_tanh"))

            def turn_out(j, l):
                br, is_v, gg = j // 4, j % 4 // 2, j % 2
                keep = is_v and br
                dst = vtok[:, br - 1, :, :] if keep else stage[:, :, :]
                if not gg and j:
                    act.wait_ge(*c.same("stored"))
                act.wait_ge(*c.take("tp_put"))
                copy(dst[:, 0:2, gg * P:(gg + 1) * P], ptr[:, 0:SEQ].rearrange("p (i d) -> p i d", i=2)).then_inc(*c.give("act_step"))
                copy(dst[0:NTS, 2, gg * P:(gg + 1) * P], ptr[0:NTS, SEQ:SEQ + P]).then_inc(*c.give("tp_got"))
                if gg:
                    act.wait_ge(*c.same("act_step"))
                    act.wait_ge(*c.same("tp_got"))
                    o_p, o_s, n = (kv_p, kv_s, br * 2 + is_v) if br < 2 else (win_p, win_s, is_v)
                    act.dma_start(o_p[bass.ds(l, 1), 0, :, n].rearrange("l (i p) g d -> p (l i) (g d)", p=P),
                                  dst[:, 0:2, :]).then_inc(*c.give("stored", 16))
                    if br < 2:
                        act.dma_start(o_s[bass.ds(l, 1), :, :, n].rearrange("l b t g d -> (l b t) (g d)"),
                                      dst[0:NTS, 2, :]).then_inc(*c.give("stored", 16))
                    else:
                        act.dma_start(o_s[bass.ds(l, 1), :, SEQ - TS:SEQ, n].rearrange("l b t g d -> (l b) t (g d)"),
                                      dst[0:NTS, 2, :]).then_inc(*c.give("stored", 16))

            with Loop(act, c, "layer", DEPTH) as l:
                c.skip("misc_put")
                c.skip("misc_got")
                split(0)
                split(1)
                act.wait_ge(*c.take("x_tile", 12))
                act.wait_ge(*c.take("x_last"))
                with Loop(act, c, "shift", 4) as i:
                    for k in mod_slots():
                        past_turned(i, k)
                for q in range(4):
                    for k in mod_slots():
                        pass
                    if q % 2:
                        act.wait_ge(*c.take("cmp_h"))
                        fn(gz[:, 0, 0:NSEQ * NBLK], cbuf[:, 1, 0:NSEQ * NBLK], ACT.Tanh, scale=0.5).then_inc(*c.give("cmp_tanh"))
                rstd()
                with Loop(act, c, "ada2", 4) as i:
                    for k in mod_slots():
                        if k == 0:
                            act.wait_ge(*c.take("h_p"))
                            act.wait_ge(*c.take("h_s"))
                            copy(h_hi[:, bass.ds(i * 4, 4), :], mix[:, bass.ds(i * 4, 4), :]).then_inc(*c.give("h_hi"))
                with Loop(act, c, "q", 2):
                    for k in range(4):
                        act.wait_ge(*c.take("tile_done"))
                        split((k + 2) % 4)
                        c.skip(f"bank{k % 2}")
                for j in range(12):
                    act.wait_ge(*c.take("tile_done"))
                    if j % 4 < 2:
                        c.skip(f"bank{j % 2}")
                    else:
                        dst = kvT[:, 2 + j % 2, :] if j < 4 else vtmp[:, j % 2, :]
                        copy(dst, proj[j % 2][:, 0:T]).then_inc(*c.give("v_ready"))
                        act.wait_ge(*c.same("v_ready"))
                        act.sem_inc(*c.give(f"bank{j % 2}"))
                    if j < 10:
                        split((j + 2) % 4)
                    elif j == 10:
                        act.wait_ge(*c.take("graw", 16))
                        for h in (slice(0, HALF), slice(HALF, KT)):
                            copy(w_hi[:, 0, h, 0:NG], graw[:, h, :]).then_inc(*c.give("hi_ready"))
                    if j:
                        turn_out(j - 1, l)
                    if j == 10:
                        hidden_tanh()
                act.wait_ge(*c.take("tile_done"))
                fn(cbuf[0:NG, 0, :], proj[0][0:NG, 0:T], ACT.Tanh, scale=0.5).then_inc(*c.give("bank0"))
                turn_out(11, l)
                c.skip("misc_put")
                c.skip("misc_got")
                hidden_tanh()
                split(0)
                split(1)
                with Loop(act, c, "turn", 2) as g:
                    for s in range(16):
                        if s == 1:
                            act.wait_ge(*c.take("tp_put"))
                            copy(vcp[:, :], ptr[0:NBLK, 0:P], scale=0.5).then_inc(*c.give("tp_got"))
                        if s in KTURN:
                            act.wait_ge(*c.take("tp_put"))
                            copy(kwork[:, 0:2, :], ptr[:, :].rearrange("p (g t) -> p g t", g=2)).then_inc(*c.give("tp_got"))
                        act.wait_ge(*c.take("tile_done"))
                        kind, ti = s // 2 % 4, s % 2
                        if kind == 0:
                            copy(cbuf[:, ti, :], proj[ti][:, 0:T]).then_inc(*c.give(f"bank{ti}"))
                        else:
                            c.skip(f"bank{ti}")
                        if kind == 2:
                            fn(gz[:, ti, :], proj[ti][:, 0:T], ACT.Tanh, scale=0.5).then_inc(*c.give("z_t"))
                        split((s + 2) % 4)
                        if s in PROMPT:
                            knd = PROMPT[s][1]
                            act.wait_ge(*c.take("sp_nm"))
                            for i in range(2):
                                w = (slice(0, P), slice(P, 3 * P))[i] if knd < 2 else slice(i * NBLK, (i + 1) * NBLK)
                                fn(prob[:, s % 2, w], pS[:, w], ACT.Exp, scale=SCALE, bias=small[:, i:i + 1],
                                   accum_out=small[:, 2 + i:3 + i]).then_inc(*c.give(("act_step", "sp_e")[i]))
                        if s - 1 in PROMPT:
                            act.wait_ge(*c.take("pt_put"))
                            w = (slice(0, P), slice(0, 3 * P)) if PROMPT[s - 1][1] < 2 else (slice(0, NBLK), slice(0, SEQ))
                            copy(probT[w], pPT[w]).then_inc(*c.give("pt_got"))
                        if s in KTURN:
                            act.wait_ge(*c.take("tp_put"))
                            copy(kwork[:, 2:4, :], ptr[:, :].rearrange("p (g t) -> p g t", g=2)).then_inc(*c.give("tp_got"))
                        if s in VTURN:
                            act.wait_ge(*c.take("tp_put"))
                            copy(vcs[:, :, :], ptr[0:NBLK, :].rearrange("p (q d) -> p q d", q=4), scale=0.5).then_inc(*c.give("tp_got"))
                        if s - 1 in SAMPLE:
                            w = T if SAMPLE[s - 1][1] < 2 else NBLK
                            act.wait_ge(*c.take("ss_nm"))
                            fn(sprob[:, 0:w], pSs[:, 0:w], ACT.Exp, scale=SCALE, bias=small[:, 4:5],
                               accum_out=small[:, 5:6]).then_inc(*c.give("ss_e"))
                        if s - 2 in SAMPLE:
                            act.wait_ge(*c.take("pts_put"))
                            if SAMPLE[s - 2][1] < 2:
                                copy(sprobT[:, 0:SEQ], pSs[:, 0:SEQ]).then_inc(*c.give("act_step"))
                                copy(sprobT[0:NTS, SEQ:3 * P], pSs[0:NTS, SEQ:3 * P]).then_inc(*c.give("act_step"))
                                act.wait_ge(*c.same("act_step"))
                                act.sem_inc(*c.give("pts_got"))
                            else:
                                copy(sprobT[0:NBLK, 0:P], pSs[0:NBLK, 0:P]).then_inc(*c.give("pts_got"))
                for k in range(8):
                    act.wait_ge(*c.take("tile_done"))
                    fn(gz[:, k % 2, :], proj[k % 2][:, 0:T], ACT.Tanh, scale=0.5).then_inc(*c.give("z_t"))
                    if k < 7:
                        split((k + 2) % 4)
                    c.skip(f"bank{k % 2}")
                for i in range(4):
                    act.wait_ge(*(c.take("ya_ready", 8) if i == 0 else c.same("ya_ready") if i == 1 else c.take("yb_ready", 4)))
                    for k in range(4 * i, 4 * i + 4):
                        fn(h_hi[:, k, :], mix[:, k, :], ACT.Identity, scale=vec[:, 64 + k:65 + k]).then_inc(
                            *c.give("act_step" if k % 4 < 3 else "y_hi"))
                split(1)
                rstd(NC_CONV, ra)
                rstd(NC_CONV)
                for half in range(2):
                    act.wait_ge(*c.take("tp_put"))
                    copy(uorow[:, half * 512:(half + 1) * 512], ptr[0:2 + 2 * NB, :]).then_inc(*c.give("tp_got"))
                act.wait_ge(*c.same("tp_got"))
                act.dma_start(conv_p[bass.ds(l, 1), 0].rearrange("l i n -> (l i) n"), uorow[0:2, :]).then_inc(*c.give("stored", 16))
                act.dma_start(conv_s[bass.ds(l, 1)].rearrange("l b i n -> (l b i) n"), uorow[2:2 + 2 * NB, :]).then_inc(
                    *c.give("stored", 16))

                def out_slot(k, t, ahead):
                    act.wait_ge(*c.take("tile_done"))
                    c.skip(f"bank{k % 2}")
                    if ahead:
                        split((k + 2) % 4)
                    act.wait_ge(*c.take("y_f"))
                    act.wait_ge(*c.take("sq_free"))
                    y = one(mix[:, bass.ds(t, 1), :])
                    fn(gz[:, k % 2, :], y, ACT.Square).then_inc(*c.give("y_sq"))
                    act.wait_ge(*c.same("y_sq"))
                    fn(y[:, 0:SEQ], y[:, 0:SEQ], ACT.Identity, scale=mod[:, bass.ds(t + 32, 1), 0]).then_inc(*c.give("act_step"))

                with Loop(act, c, "out", 3) as i:
                    for k in range(4):
                        if k == 2:
                            act.wait_ge(*c.same("stored"))
                        out_slot(k, i * 4 + k, True)
                for k in range(4):
                    out_slot(k, 12 + k, k < 2)
                rstd()
            for k in range(0, KT, 2):
                act.wait_ge(*c.take("fin_put0"))
                copy(yp[:, :, k * P:(k + 1) * P], proj[0][:, 0:SEQ].rearrange("p (i n) -> p i n", i=2)).then_inc(*c.give("act_step"))
                copy(ys[:, k * P:(k + 1) * P], proj[0][0:NTS, SEQ:SEQ + P]).then_inc(*c.give("bank0"))
                if k % (KT // 2) == KT // 2 - 2:
                    half = slice((k + 2 - KT // 2) * P, (k + 2) * P)
                    c.skip("bank1", KT // 4)
                    act.wait_ge(*c.same("act_step"))
                    act.wait_ge(*c.same("bank0"))
                    act.wait_ge(*c.same("bank1"))
                    for i in range(2):
                        act.dma_start(y_p[0, i * P:(i + 1) * P, half], yp[:, i, half]).then_inc(*c.give("stored", 16))
                    act.dma_start(y_s.rearrange("b t d -> (b t) d")[:, half], ys[:, half]).then_inc(*c.give("stored", 16))
            act.wait_ge(*c.same("stored"))

        @block.vector
        def _(dve):
            c = Counts(dve, sems, per.setdefault("dve", {}))
            tt, ts, stt, cp = nc.vector.tensor_tensor, nc.vector.tensor_scalar, nc.vector.scalar_tensor_tensor, nc.vector.tensor_copy

            def link(ins):
                ins.then_inc(*c.give("dve_step"))
                dve.wait_ge(*c.same("dve_step"))

            nc.vector.memset(ones[:, :], 1.0).then_inc(*c.give("bank0"))
            for i in range(2):
                nc.vector.memset(past[i][:, 16, :], 0.0).then_inc(*c.give("dve_step" if i else "bank1"))
            nc.vector.memset(eps, EPS).then_inc(*c.give("misc_got"))
            nc.vector.memset(qs[:, :, :], 0.0).then_inc(*c.give("dve_step"))
            nc.vector.memset(small[:, 0:15], 0.0).then_inc(*c.give("mem_set"))
            dve.sem_inc(*c.give("lo_ready", 8))
            dve.wait_ge(*c.take("c_tanh"))
            stt(mixf[0:ROWS, 0:DM], mixf[0:ROWS, 0:DM], 1.0, mixf[0:ROWS, DM:2 * DM], ALU.add, ALU.mult).then_inc(*c.give("c_done"))
            dve.wait_ge(*c.take("misc_put"))
            cF = gz[:, 0, 0:KT * ROWS].rearrange("p (k r) -> p k r", k=KT)
            ts(cF, pmisc[:, 0:KT * ROWS].rearrange("p (k r) -> p k r", k=KT), 0.5, None, ALU.mult).then_inc(*c.give("misc_got"))
            dve.wait_ge(*c.same("misc_got"))
            link(cp(cHL[:, :, 0:ROWS], cF))
            tt(cHL[:, :, ROWS:2 * ROWS], cF, cHL[:, :, 0:ROWS].bitcast(F32), ALU.subtract).then_inc(*c.give("dve_step"))
            for k in range(0, KT, 2):
                dve.wait_ge(*c.take("x_put0"))
                cp(xv[:, k, :], proj[0][:, 0:T]).then_inc(*c.give("bank0"))
            c.skip("bank1", KT // 2)
            dve.wait_ge(*c.same("bank0"))
            dve.wait_ge(*c.same("bank1"))
            dve.sem_inc(*c.give("x_tile", 12))
            dve.sem_inc(*c.give("op_got"))
            dve.sem_inc(*c.give("os_got"))
            c.skip("sp_e")

            def split(k):
                s = k % 2
                for h in (slice(0, HALF), slice(HALF, KT)):
                    dve.wait_ge(*c.take("hi_ready"))
                    tt(w_lo[:, s, h, :], rawv[k // 2 % 2][:, h, s * P:(s + 1) * P], w_hi[:, s, h, :].bitcast(F32),
                       ALU.subtract).then_inc(*c.give("lo_ready"))

            def mod_slots(i, base):
                for k in range(4):
                    dve.wait_ge(*c.take("tile_done"))
                    split((k + 2) % 4)
                    yield k
                dve.wait_ge(*c.take("misc_put"))
                j = i * 4 + base
                tt(mod[:, bass.ds(j, 4), :], pmisc[:, 0:4 * ROWS].rearrange("p (k r) -> p k r", k=4),
                   vec[:, bass.ds(j, 4)].unsqueeze(2).to_broadcast([P, 4, ROWS]), ALU.add).then_inc(*c.give("misc_got"))

            def invert(r, done="dve_step"):
                dve.wait_ge(*c.take("misc_got"))
                nc.vector.reciprocal(r[:, :], r[:, :]).then_inc(*c.give(done))
                dve.wait_ge(*c.same(done))

            def rope(src, dst):
                half = HD // 2
                t = ubuf[:, 0, 0:T]
                tt(t[half:P], src[0:half], cst[0:half, C_SIN:C_SIN + T], ALU.mult).then_inc(*c.give("dve_step"))
                tt(t[0:half], src[half:P], cst[half:P, C_SIN:C_SIN + T], ALU.mult).then_inc(*c.give("dve_step"))
                link(tt(dst, src, cst[:, C_COS:C_COS + T], ALU.mult))
                return tt(dst, dst, t, ALU.add)

            def one(ap):
                return ap.rearrange("p a t -> p (a t)")

            samp = lambda ap: ap.rearrange("p k (b t) -> p k b t", t=TS)

            def conv_slot(s, g):
                kind, ti = s // 2 % 4, s % 2
                out, bank = proj[ti][:, 0:T], f"bank{ti}"
                u = ubuf[:, ti, :]
                us = u[:, 2 + SEQ:].rearrange("p (b t) -> p b t", b=NB)
                cs = cbuf[:, ti, SEQ:T].rearrange("p (b t) -> p b t", b=NB)
                tile = 2 * (s // 8) + ti
                if kind == 0:
                    c.skip(bank)
                elif kind == 1:
                    tt(u[:, 2:2 + SEQ], out[:, 0:SEQ], cbuf[:, ti, 0:SEQ], ALU.mult).then_inc(*c.give("dve_step"))
                    cp(us[:, :, 0:2], one(stT[:, bass.ds(g * 4 + tile, 1), :]).rearrange("p (b i) -> p b i", b=NB)).then_inc(
                        *c.give("dve_step"))
                    tt(us[:, :, 2:], out[:, SEQ:T].rearrange("p (b t) -> p b t", b=NB), cs, ALU.mult).then_inc(*c.give(bank))
                    dve.wait_ge(*c.same("dve_step"))
                    dve.wait_ge(*c.same(bank))
                    un = one(uo[:, bass.ds(g * 4 + tile, 1), :])
                    cp(un[:, 0:2], u[:, SEQ:SEQ + 2]).then_inc(*c.give("dve_step"))
                    cp(un[:, 2:].rearrange("p (b i) -> p b i", b=NB), us[:, :, TS:]).then_inc(*c.give("dve_step"))
                    for i in range(3):
                        w = vec[:, bass.ds(g * 4 + (96 + 8 * i + tile), 1)]
                        if i == 0:
                            ts(cbuf[:, ti, 0:SEQ], u[:, 0:SEQ], w, None, ALU.mult).then_inc(*c.give("dve_step"))
                            link(ts(cs, us[:, :, 0:TS], w, None, ALU.mult))
                        else:
                            stt(cbuf[:, ti, 0:SEQ], u[:, i:i + SEQ], w, cbuf[:, ti, 0:SEQ], ALU.mult, ALU.add).then_inc(
                                *c.give("dve_step"))
                            link(stt(cs, us[:, :, i:i + TS], w, cs, ALU.mult, ALU.add))
                elif kind == 2:
                    dve.wait_ge(*c.take("z_t"))
                    stt(gz[:, ti, :], gz[:, ti, :], 1.0, out, ALU.add, ALU.mult).then_inc(*c.give(bank))
                else:
                    ya = one(mix[:, bass.ds(g * 4 + tile, 1), :])
                    stt(ya, out, 0.5, cbuf[:, ti, :], ALU.mult, ALU.mult).then_inc(*c.give(bank))
                    dve.wait_ge(*c.same(bank))
                    tt(ya, ya, gz[:, ti, :], ALU.mult).then_inc(*c.give("ya_ready"))

            def hidden(i, n, dst, at=0):
                dve.wait_ge(*c.take("cmp_put"))
                if at == 0:
                    link(cp(small[:, 12 + i:13 + i], pSs[:, (NSEQ * NBLK + 2 * i):(NSEQ * NBLK + 2 * i + 1)]))
                src, got = pSs[:, 0:n], cbuf[:, 1, 0:n]
                if at:
                    src = (pSs, pPT)[i][:, at:at + 2 * T // STRIDE].rearrange("p (g n) -> p g n", g=2)[:, :, 0:NBLK]
                    got = got.rearrange("p (g n) -> p g n", g=2)
                ts(got, src, small[:, 12 + i:13 + i], None, ALU.add).then_inc(*c.give("cmp_h"))
                dve.wait_ge(*c.take("cmp_tanh"))
                link(stt(dst, gz[:, 0, 0:n], 1.0, cbuf[:, 1, 0:n], ALU.add, ALU.mult))

            with Loop(dve, c, "layer", DEPTH) as l:
                dve.wait_ge(*c.take("misc_put"))
                link(cp(vec[:, :], pmisc[:, 0:120]))
                dve.wait_ge(*c.take("x_last"))
                for i in range(2):
                    link(cp(past[i][:, 16, 0:64], pmisc[:, 128:192]))
                cp(stT[:, :, :], pmisc[:, 192:320].rearrange("p (k r) -> p k r", k=8)).then_inc(*c.give("misc_got"))
                split(0)
                split(1)
                with Loop(dve, c, "shift", 4) as i:
                    for k in mod_slots(i, 0):
                        pass
                for q in range(4):
                    for k in mod_slots(0, 16 + 4 * q):
                        pass
                    if q % 2:
                        hidden(q // 2, NSEQ * NBLK, cact[:, q // 2, 0:NSEQ * NBLK])
                dve.wait_ge(*c.same("misc_got"))
                c.skip("misc_put")
                link(stt(mod[:, 16:32, :], mod[:, 16:32, :], 1.0, vec[:, 48:64].unsqueeze(2).to_broadcast([P, 16, ROWS]),
                         ALU.add, ALU.mult))
                invert(rs, "rs_ready")
                with Loop(dve, c, "ada2", 4) as i:
                    for k in mod_slots(i, 32):
                        if k == 1:
                            dve.wait_ge(*c.take("h_hi"))
                            tt(h_lo[:, bass.ds(i * 4, 4), :], mix[:, bass.ds(i * 4, 4), :],
                               h_hi[:, bass.ds(i * 4, 4), :].bitcast(F32), ALU.subtract).then_inc(*c.give("h_ready"))
                dve.wait_ge(*c.same("misc_got"))
                link(tt(mod[:, 32:48, :], mod[:, 32:48, :], vec[:, 80:96].unsqueeze(2).to_broadcast([P, 16, ROWS]), ALU.mult))
                with Loop(dve, c, "q", 2) as i:
                    for k in range(4):
                        dve.wait_ge(*c.take("tile_done"))
                        rope(proj[k % 2][:, 0:T], one(mix[:, bass.ds(i * 4 + (8 + k), 1), :])).then_inc(*c.give(f"bank{k % 2}"))
                        dve.wait_ge(*c.same(f"bank{k % 2}"))
                        split((k + 2) % 4)
                for j in range(12):
                    dve.wait_ge(*c.take("tile_done"))
                    if j % 4 < 2:
                        rope(proj[j % 2][:, 0:T], kvT[:, (0, 4, 6)[j // 4] + j % 4, :]).then_inc(*c.give("kv_done"))
                        dve.wait_ge(*c.same("kv_done"))
                        dve.sem_inc(*c.give(f"bank{j % 2}"))
                    else:
                        c.skip(f"bank{j % 2}")
                    if j < 10:
                        split((j + 2) % 4)
                    elif j == 10:
                        for h in (slice(0, HALF), slice(HALF, KT)):
                            dve.wait_ge(*c.take("hi_ready"))
                            tt(w_lo[:, 0, h, 0:NG], graw[:, h, :], w_hi[:, 0, h, 0:NG].bitcast(F32), ALU.subtract).then_inc(
                                *c.give("lo_ready"))
                    if j in (8, 11):
                        i = j // 11
                        dve.wait_ge(*c.take("cmp_put"))
                        cp(gz[0:NROW, 1, i * P:(i + 1) * P], (pSs, pPT)[i][0:NROW, 0:P]).then_inc(*c.give("cmp_row"))
                    if j == 10:
                        hidden(0, 2 * NBLK, cact[:, 0, NSEQ * NBLK:(NSEQ + 2) * NBLK], 256)
                dve.wait_ge(*c.take("tile_done"))
                dve.wait_ge(*c.take("bank0"))
                link(ts(cbuf[0:NG, 0, :], cbuf[0:NG, 0, :], 0.5, 0.5, ALU.mult, ALU.add))
                gx = ubuf[0:NG, :, :].rearrange("p a b -> p (a b)")
                for p in range(4):
                    last = cp(gx[:, p * P:(p + 1) * P].rearrange("p (b r t) -> p b r t", b=2, t=TS),
                              cbuf[0:NG, 0, SEQ + 8 * p:SEQ + 8 * p + 8].rearrange("p (b t) -> p b t", b=2).unsqueeze(2).to_broadcast(
                                  [NG, 2, 16, TS])).then_inc(*c.give("dve_step" if p < 3 else "gate_ready"))
                dve.wait_ge(*c.take("misc_put"))
                cp(gtok[:, :, :], pmisc[:, 0:2 * NG].rearrange("p (i n) -> p i n", i=2)).then_inc(*c.give("dve_step"))
                gm = ubuf[:, 0, 0:4 * NG]
                tt(gm.rearrange("p (q n) -> p q n", q=4), pmisc[:, 48:48 + 4 * NG].rearrange("p (q n) -> p q n", q=4),
                   cst[:, C_GM:C_GM + NG].unsqueeze(1).to_broadcast([P, 4, NG]), ALU.mult).then_inc(*c.give("misc_got"))
                dve.wait_ge(*c.same("misc_got"))
                link(nc.vector.tensor_reduce(gsm[:, :, :], gm.rearrange("p (q h b) -> p q b h", q=4, b=3), AX_X, ALU.add))
                link(nc.vector.memset(ubuf[:, :, 0:2], 0.0))

                hidden(1, 2 * NBLK, cact[:, 1, NSEQ * NBLK:(NSEQ + 2) * NBLK], 256)
                dve.sem_inc(*c.give("cmp_a"))
                split(0)
                dve.wait_ge(*c.take("kc_put"))
                ts(kcT[:, :], pSs[:, 0:(NSEQ + 2) * NBLK], 0.5, None, ALU.mult).then_inc(*c.give("kc_got"))
                split(1)

                with Loop(dve, c, "turn", 2) as g:
                    for s in range(16):
                        if s - 5 in (0, 3, 6, 9):
                            dve.wait_ge(*c.take("op_put"))
                            cp(one(mix[:, bass.ds(g * 4 + (8 + (s - 5) // 3), 1), 0:SEQ]), pO[:, 0:SEQ]).then_inc(*c.give("op_got"))
                        if s in (8, 15):
                            pp = int(s == 15)
                            dve.wait_ge(*c.take("os_put"))
                            for q in range(4):
                                cp(mix[:, 8 + (q % 2) * 4:12 + (q % 2) * 4, bass.ds(g * 16 + (SEQ + 8 * pp + 4 * (q // 2)), TS)],
                                   pOs[:, q * 16:(q + 1) * 16].rearrange("p (r t) -> p r t", r=4)).then_inc(
                                       *c.give("dve_step" if q < 3 else "os_got"))
                        if s - 1 in PROMPT:
                            head, kind = PROMPT[s - 1]
                            pr = prob[:, (s - 1) % 2, :]
                            dve.wait_ge(*c.take("sp_e"))
                            if kind == 2:
                                link(ts(small[:, 2:4], small[:, 2:4], 1e-30, None, ALU.max))
                            link(nc.vector.reciprocal(small[:, 6:8], small[:, 2:4]))
                            gcol = gtok[:, :, bass.ds(g * 12 + (3 * head + GATE[kind]), 1)].rearrange("p i a -> p (i a)")
                            link(tt(small[:, 6:8], small[:, 6:8], gcol, ALU.mult))
                            if kind < 2:
                                ts(pr[:, 0:P], pr[:, 0:P], small[:, 6:7], None, ALU.mult).then_inc(*c.give("dve_step"))
                                ts(pr[:, P:3 * P], pr[:, P:3 * P], small[:, 7:8], None, ALU.mult).then_inc(*c.give("sp_p"))
                            else:
                                pv = pr[:, 0:2 * NBLK].rearrange("p (i n) -> p i n", i=2)
                                tt(pv, pv, small[:, 6:8].unsqueeze(2).to_broadcast([P, 2, NBLK]), ALU.mult).then_inc(*c.give("sp_p"))
                        if s - 2 in SAMPLE:
                            pp, kind = SAMPLE[s - 2]
                            w = T if kind < 2 else NBLK
                            dve.wait_ge(*c.take("ss_e"))
                            link(nc.vector.reciprocal(small[:, 8:9], small[:, 5:6]))
                            gcol = gsm[:, bass.ds(g * 2 + pp, 1), GATE[kind]]
                            link(tt(small[:, 8:9], small[:, 8:9], gcol, ALU.mult))
                            ts(sprob[:, 0:w], sprob[:, 0:w], small[:, 8:9], None, ALU.mult).then_inc(*c.give("ss_p"))
                        dve.wait_ge(*c.take("tile_done"))
                        conv_slot(s, g)
                        if s not in PROMPT:
                            split((s + 2) % 4)
                        if s in PROMPT:
                            kind = PROMPT[s][1]
                            dve.wait_ge(*c.take("sp_put"))
                            if kind < 2:
                                link(tt(pS[:, 0:P], pS[:, 0:P], tri, ALU.add))
                                link(tt(pS[:, 2 * P:3 * P], pS[:, 2 * P:3 * P], tri, ALU.add))
                                nc.vector.tensor_reduce(small[:, 9:10], pS[:, 0:P], AX_X, ALU.max).then_inc(*c.give("dve_step"))
                                link(nc.vector.tensor_reduce(small[:, 10:11], pS[:, P:3 * P], AX_X, ALU.max))
                                ts(small[:, 0:2], small[:, 9:11], -SCALE, None, ALU.mult).then_inc(*c.give("sp_nm"))
                            else:
                                link(tt(pS[:, 0:2 * NBLK], pS[:, 0:2 * NBLK], cst[:, C_CMP:C_CMP + 2 * NBLK], ALU.add))
                                link(nc.vector.tensor_reduce(small[:, 9:11], pS[:, 0:2 * NBLK].rearrange("p (i n) -> p i n", i=2),
                                                             AX_X, ALU.max))
                                ts(small[:, 0:2], small[:, 9:11], -1e29, -SCALE, ALU.max, ALU.mult).then_inc(*c.give("sp_nm"))
                            split((s + 2) % 4)
                        if s - 1 in SAMPLE:
                            pp, kind = SAMPLE[s - 1]
                            w = T if kind < 2 else NBLK
                            dve.wait_ge(*c.take("ss_put"))
                            if kind < 2:
                                link(tt(pSs[:, SEQ:T], pSs[:, SEQ:T], cst[:, bass.ds(g * (2 * NTS) + (C_NEW + pp * NTS), NTS)], ALU.add))
                            link(nc.vector.tensor_reduce(small[:, 11:12], pSs[:, 0:w], AX_X, ALU.max))
                            ts(small[:, 4:5], small[:, 11:12], -SCALE, None, ALU.mult).then_inc(*c.give("ss_nm"))
                dve.wait_ge(*c.same("dve_step"))
                dve.sem_inc(*c.give("u_put"))
                for k in range(8):
                    dve.wait_ge(*c.take("tile_done"))
                    dve.wait_ge(*c.take("z_t"))
                    stt(gz[:, k % 2, :], gz[:, k % 2, :], 1.0, proj[k % 2][:, 0:T], ALU.add, ALU.mult).then_inc(*c.give(f"bank{k % 2}"))
                    dve.wait_ge(*c.same(f"bank{k % 2}"))
                    stt(mix[:, 8 + k, :], mix[:, 8 + k, :], 0.5, gz[:, k % 2, :], ALU.mult, ALU.mult).then_inc(*c.give("yb_ready"))
                    if k < 7:
                        split((k + 2) % 4)
                for i in range(4):
                    dve.wait_ge(*c.take("y_hi"))
                    for k in range(4 * i, 4 * i + 4):
                        stt(h_lo[:, k, :], mix[:, k, :], vec[:, 64 + k:65 + k], h_hi[:, k, :].bitcast(F32),
                            ALU.mult, ALU.subtract).then_inc(*c.give("dve_step" if k % 4 < 3 else "y_hl"))
                split(1)
                c.skip("misc_put", 2)
                invert(ra)
                invert(rs)

                def out_slot(k, t, ahead):
                    dve.wait_ge(*c.take("tile_done"))
                    y = one(mix[:, bass.ds(t, 1), :])
                    tt(y, proj[k % 2][:, 0:T], ra[:, :], ALU.mult).then_inc(*c.give("dve_step"))
                    tt(cbuf[:, k % 2, :], pB[k % 2][:, 0:T], rs[:, :], ALU.mult).then_inc(*c.give(f"bank{k % 2}"))
                    dve.wait_ge(*c.same("dve_step"))
                    dve.wait_ge(*c.same(f"bank{k % 2}"))
                    tt(y, y, cbuf[:, k % 2, :], ALU.add).then_inc(*c.give("y_f"))
                    if ahead:
                        split((k + 2) % 4)

                with Loop(dve, c, "out", 3) as i:
                    for k in range(4):
                        out_slot(k, i * 4 + k, True)
                for k in range(4):
                    out_slot(k, 12 + k, k < 2)
                c.skip("misc_put")
                invert(rs, "rs_ready")
                dve.wait_ge(*c.take("x_back", 16))
                for i in range(3):
                    y4, x4 = mix[:, i * 4:i * 4 + 4, :], xv[:, i * 4:i * 4 + 4, :]
                    link(tt(y4, y4, rs[:, :].unsqueeze(1).to_broadcast([P, 4, T]), ALU.mult))
                    tt(x4, x4, y4, ALU.add).then_inc(*c.give("x_tile", 4))

            for k in range(1, KT, 2):
                dve.wait_ge(*c.take("fin_put1"))
                cp(yp[:, :, k * P:(k + 1) * P], proj[1][:, 0:SEQ].rearrange("p (i n) -> p i n", i=2)).then_inc(*c.give("dve_step"))
                cp(ys[:, k * P:(k + 1) * P], proj[1][0:NTS, SEQ:SEQ + P]).then_inc(*c.give("bank1"))

        @block.gpsimd
        def _(pool):
            c = Counts(pool, sems, per.setdefault("pool", {}))
            tt, cp = nc.gpsimd.tensor_tensor, nc.gpsimd.tensor_copy

            def link(ins):
                ins.then_inc(*c.give("pool_step"))
                pool.wait_ge(*c.same("pool_step"))

            def square(src, done=None, acc=acc):
                link(tt(sqp[:, :], src, src, ALU.mult))
                last = tt(acc[:, :], acc[:, :], sqp[:, :], ALU.add)
                if done:
                    last.then_inc(*c.give(done))
                    pool.wait_ge(*c.same(done))
                else:
                    link(last)

            def one(ap):
                return ap.rearrange("p a t -> p (a t)")

            samp = lambda ap: ap.rearrange("p k (b t) -> p k b t", t=TS)

            def squares_of_x():
                with Loop(pool, c, "xsq", 3) as i:
                    pool.wait_ge(*c.take("x_tile", 4))
                    for k in range(4):
                        square(one(xv[:, bass.ds(i * 4 + k, 1), :]))
                for k in range(12, 16):
                    square(xv[:, k, :], "ssq_ready" if k == 15 else None)

            link(nc.gpsimd.memset(sqp[:, :], 0.0))
            link(nc.gpsimd.memset(accb[:, :], 0.0))
            pool.wait_ge(*c.ahead("x_tile", 12))
            nc.gpsimd.memset(acc[:, :], 0.0).then_inc(*c.give("sq_free", 2))
            pool.wait_ge(*c.same("sq_free"))
            pool.sem_inc(*c.give("x_last"))
            c.skip("misc_got", 2)
            with Loop(pool, c, "layer", DEPTH) as l:
                squares_of_x()
                c.skip("misc_got", 9)
                pool.wait_ge(*c.take("misc_got"))
                apart(pool)
                link(nc.gpsimd.memset(acc[:, :], 0.0))
                pool.wait_ge(*c.take("rs_ready"))
                with Loop(pool, c, "norm", 4) as i:
                    m4 = mix[:, bass.ds(i * 4, 4), :]
                    tt(m4, xv[:, bass.ds(i * 4, 4), :], rs[:, :].unsqueeze(1).to_broadcast([P, 4, T]), ALU.mult).then_inc(
                        *c.give("xn"))
                    pool.wait_ge(*c.same("xn"))
                    m4p = mix[:, bass.ds(i * 4, 4), 0:SEQ]
                    tt(m4p, m4p, mod[:, bass.ds(i * 4 + 16, 4), 0:1].to_broadcast([P, 4, SEQ]), ALU.mult).then_inc(*c.give("pool_step"))
                    m4s = samp(mix[:, bass.ds(i * 4, 4), SEQ:T])
                    link(tt(m4s, m4s, mod[:, bass.ds(i * 4 + 16, 4), 1:ROWS].unsqueeze(3).to_broadcast([P, 4, NB, TS]), ALU.mult))
                    tt(m4p, m4p, mod[:, bass.ds(i * 4, 4), 0:1].to_broadcast([P, 4, SEQ]), ALU.add).then_inc(*c.give("h_p"))
                    tt(m4s, m4s, mod[:, bass.ds(i * 4, 4), 1:ROWS].unsqueeze(3).to_broadcast([P, 4, NB, TS]),
                       ALU.add).then_inc(*c.give("h_s"))
                c.skip("misc_got", 5)
                pool.wait_ge(*c.take("kc_got"))
                with Loop(pool, c, "turn", 2) as g:
                    def pass_copies(pp):
                        for q in range(4):
                            cp(qs[:, q, 0:16].rearrange("p (r t) -> p r t", r=4),
                               mix[:, 8 + (q % 2) * 4:12 + (q % 2) * 4, bass.ds(g * 16 + (SEQ + 8 * pp + 4 * (q // 2)), TS)]).then_inc(
                                   *c.give("pool_step" if q < 3 else "qs_ready"))
                        cp(avc[:, 5 * NBLK:9 * NBLK], kcT[:, bass.ds(g * (8 * NBLK) + pp * 4 * NBLK, 4 * NBLK)]).then_inc(
                            *c.give("pool_step"))
                        cp(avc[:, 0:4 * NBLK], cact[:, 1, bass.ds(g * (8 * NBLK) + pp * 4 * NBLK, 4 * NBLK)]).then_inc(*c.give("av_ready"))

                    def query(h):
                        cp(qc[:, h % 2, :], one(mix[:, bass.ds(g * 4 + (8 + h), 1), 0:SEQ])).then_inc(*c.give("qc_ready"))

                    query(0)
                    pass_copies(0)
                    for br in range(2):
                        cp(vcur[:, br, :, :], vtok[:, br, 0:2, bass.ds(g * P, P)]).then_inc(*c.give("pool_step"))
                    cp(avc[:, 4 * NBLK:5 * NBLK], cact[:, 1, bass.ds(g * NBLK + NSEQ * NBLK, NBLK)]).then_inc(*c.give("v_turn"))
                    query(1)
                    pool.wait_ge(*c.take("op_put"))
                    query(2)
                    pool.wait_ge(*c.take("op_put"))
                    query(3)
                    apart(pool)
                    for b in range(NB // 2):
                        pool.dma_start(win_s[bass.ds(l, 1), bass.ds(g * (NB // 2) + b, 1), 0:SEQ - TS].rearrange(
                            "l b t c g d -> (l b t) (c g d)"), cache_win[bass.ds(l, 1), bass.ds(g * (NB // 2) + b, 1), TS:SEQ].rearrange(
                                "l b t c g d -> (l b t) (c g d)")).then_inc(*c.give("stored2", 16))
                    pool.wait_ge(*c.take("os_put"))
                    pass_copies(1)
                    for m in range(2):
                        for ti in range(2):
                            pool.wait_ge(*c.take("ya_ready"))
                            square(one(mix[:, bass.ds(g * 4 + (2 * m + ti), 1), :]))
                    c.skip("op_put", 2)
                    pool.wait_ge(*c.take("os_put"))
                pool.sem_inc(*c.give("a_done"))
                with Loop(pool, c, "z", 2) as i:
                    for k in range(4):
                        pool.wait_ge(*c.take("yb_ready"))
                        square(one(mix[:, bass.ds(i * 4 + (8 + k), 1), :]), acc=accb)
                pool.sem_inc(*c.give("b_done"))
                pool.wait_ge(*c.take("misc_got", 2))
                apart(pool)
                nc.gpsimd.memset(acc[:, :], 0.0).then_inc(*c.give("pool_step"))
                link(nc.gpsimd.memset(accb[:, :], 0.0))
                with Loop(pool, c, "out", 4) as i:
                    for k in range(4):
                        pool.wait_ge(*c.take("y_sq"))
                        tt(acc[:, :], acc[:, :], gz[:, k % 2, :], ALU.add).then_inc(*c.give("sq_free"))
                        pool.wait_ge(*c.same("sq_free"))
                        ys = one(mix[:, bass.ds(i * 4 + k, 1), SEQ:T]).rearrange("p (b t) -> p b t", t=TS)
                        gate = one(mod[:, bass.ds(i * 4 + (32 + k), 1), 1:ROWS])
                        tt(ys, ys, gate.unsqueeze(2).to_broadcast([P, NB, TS]), ALU.mult).then_inc(*c.give("pool_step"))
                pool.wait_ge(*c.same("pool_step"))
                pool.sem_inc(*c.give("y_done"))
                pool.wait_ge(*c.take("misc_got"))
                apart(pool)
                link(nc.gpsimd.memset(acc[:, :], 0.0))
                pool.wait_ge(*c.take("rs_ready"))
                pool.wait_ge(*c.take("x_back", 16))
                link(tt(mix[:, 12:16, :], mix[:, 12:16, :], rs[:, :].unsqueeze(1).to_broadcast([P, 4, T]), ALU.mult))
                tt(xv[:, 12:16, :], xv[:, 12:16, :], mix[:, 12:16, :], ALU.add).then_inc(*c.give("x_last"))
                pool.wait_ge(*c.same("x_last"))
            pool.wait_ge(*c.same("stored2"))


_INS = ["x_prompt", "x_sample", "cache_kv", "cache_win", "state_conv", "page_table", "c_prompt", "c_sample", "w_ada",
        "b_ada", "g_pre", "w_in", "conv_w", "cmp_pe", "cmp_w1", "cmp_w2", "g_grp", "w_out", "g_post"]
_OUTS = [(1, SEQ, DM), (NB, TS, DM), (DEPTH, 1, SEQ, 4, NKV, HD), (DEPTH, NB, TS, 4, NKV, HD), (DEPTH, 1, SEQ, 2, NKV, HD),
         (DEPTH, NB, SEQ, 2, NKV, HD), (DEPTH, 1, 2, NC_CONV), (DEPTH, NB, 2, NC_CONV)]


def kernel(**inputs):
    import concourse.bacc as bacc
    from concourse.bass_utils import run_bass_kernel_spmd as run

    arrays = {f"in_{n}": np.ascontiguousarray(inputs[n]) for n in _INS}
    arrays["in_shape_constants"] = shape_constants()
    per = {}
    for final in (False, True):
        nc = bacc.Bacc("TRN2", target_bir_lowering=False, num_devices=1)
        ins = [nc.dram_tensor(n, a.shape, mybir.dt.from_np(a.dtype), kind="ExternalInput").ap() for n, a in arrays.items()]
        outs = [nc.dram_tensor(f"out_{i}", s, F32, kind="ExternalOutput").ap() for i, s in enumerate(_OUTS)]
        spill = nc.dram_tensor("x_scratch", (P, KT * T), F32, kind="Internal").ap()
        program(nc, per, ins[:-1], outs, ins[-1], spill)
        per_layer = {}
        for counts in per.values():
            for (name, loop), k in counts.items():
                if loop == "layer":
                    assert per_layer.setdefault(name, k) == k, (name, per_layer[name], k)
    r = run(nc, [arrays], core_ids=[0])
    return tuple(r.results[0][f"out_{i}"] for i in range(len(_OUTS)))
```
